# Optimizing a Trainium2 kernel written in Bass

```python
import math
import jax
import jax.numpy as jnp
from jax import lax
import numpy as np
import jax, jax.numpy as jnp

D_MODEL = 1024
BATCH = 1
SEQ = 256
DEPTH = 2

GRID_W = 64
CTX_LEN = 256
EPS = 1e-6
N_MOD = 6

DN_QK_HEADS = 8
DN_V_HEADS = 16
DN_HEAD_DIM = 128
DN_REP = DN_V_HEADS // DN_QK_HEADS
DN_KEY_W = DN_QK_HEADS * DN_HEAD_DIM
DN_VAL_W = DN_V_HEADS * DN_HEAD_DIM
DN_CONV_W = 2 * DN_KEY_W + DN_VAL_W
DN_IN_W = DN_CONV_W + DN_VAL_W + 4 * DN_V_HEADS
DN_CONV = 5
DN_CHUNK = 64

ATT_Q_HEADS = 8
ATT_KV_HEADS = 2
ATT_GROUP = ATT_Q_HEADS // ATT_KV_HEADS
ATT_HEAD_DIM = 128
ATT_Q_W = ATT_Q_HEADS * ATT_HEAD_DIM
ATT_KV_W = ATT_KV_HEADS * ATT_HEAD_DIM
ATT_IN_W = ATT_Q_W + 2 * ATT_KV_W
ATT_BLOCK = 128
ROPE_THETA = 10000.0

PEER_HEADS = 8
PEER_N_KEYS = 128
PEER_N_EXPERTS = PEER_N_KEYS * PEER_N_KEYS
PEER_QUERY_DIM = 256
PEER_HALF = PEER_QUERY_DIM // 2
PEER_TOPK = 16
PEER_TOKEN_BLOCK = 128

N_DN_LAYERS = (DEPTH + 1) // 2
N_ATT_LAYERS = DEPTH // 2


def rmsnorm(x, gain):
    xf = x.astype(jnp.float32)
    y = xf * lax.rsqrt(jnp.mean(xf * xf, axis=-1, keepdims=True) + EPS)
    return (y * gain.astype(jnp.float32)).astype(x.dtype)

def l2norm(x):
    xf = x.astype(jnp.float32)
    return xf * lax.rsqrt(jnp.sum(xf * xf, axis=-1, keepdims=True) + EPS)

def ada_params(cond, w, b):
    return jnp.split((cond @ w + b)[:, None, :], N_MOD, axis=-1)

def axial_rope_tables(n_tokens):
    rows = n_tokens // GRID_W
    row = jnp.broadcast_to(jnp.arange(rows)[:, None], (rows, GRID_W)).reshape(-1).astype(jnp.float32)
    col = jnp.broadcast_to(jnp.arange(GRID_W)[None, :], (rows, GRID_W)).reshape(-1).astype(jnp.float32)
    axis_dim = ATT_HEAD_DIM // 2
    freqs = ROPE_THETA ** (-jnp.arange(0, axis_dim, 2, dtype=jnp.float32) / axis_dim)
    ang = jnp.concatenate([row[:, None] * freqs, col[:, None] * freqs], axis=-1)
    return jnp.cos(ang), jnp.sin(ang)

def apply_rope(x, cos, sin):
    xf = x.astype(jnp.float32).reshape(x.shape[:-1] + (x.shape[-1] // 2, 2))
    x1, x2 = xf[..., 0], xf[..., 1]
    c = cos[None, :, None, :]
    s = sin[None, :, None, :]
    return jnp.stack([x1 * c - x2 * s, x1 * s + x2 * c], axis=-1).reshape(x.shape).astype(x.dtype)

def centred_dwconv(x, w):
    p = w.shape[0] // 2
    return lax.conv_general_dilated(x, w[:, None, :].astype(x.dtype), window_strides=(1,), padding=[(p, p)],
                                    dimension_numbers=('NWC', 'WIO', 'NWC'), feature_group_count=x.shape[-1])

def gated_delta_chunked(q, k, v, g, beta, s0):
    B, T, H, _ = q.shape
    dv = v.shape[-1]
    n = T // DN_CHUNK

    def chunkify(a):
        a = a.reshape((B, n, DN_CHUNK, H) + a.shape[3:])
        return jnp.moveaxis(a, (1, 3), (0, 2))

    incl = jnp.tril(jnp.ones((DN_CHUNK, DN_CHUNK), dtype=bool))
    strict = jnp.tril(jnp.ones((DN_CHUNK, DN_CHUNK), dtype=bool), -1)
    eye = jnp.eye(DN_CHUNK, dtype=jnp.float32)

    def step(S, inp):
        qc, kc, vc, gc, bc = inp
        gc = jnp.cumsum(gc, axis=-1)
        decay = jnp.exp(jnp.where(incl, gc[..., :, None] - gc[..., None, :], -jnp.inf))
        kk = jnp.einsum('bhid,bhjd->bhij', kc, kc)
        a = eye + jnp.where(strict, kk * decay * bc[..., :, None], 0.0)
        rhs = jnp.concatenate([vc * bc[..., None], kc * (bc * jnp.exp(gc))[..., None]], axis=-1)
        sol = lax.linalg.triangular_solve(a, rhs, left_side=True, lower=True, unit_diagonal=True)
        u, w = sol[..., :dv], sol[..., dv:]
        v_new = u - jnp.einsum('bhcd,bhde->bhce', w, S)
        qk = jnp.where(incl, jnp.einsum('bhid,bhjd->bhij', qc, kc) * decay, 0.0)
        o = (jnp.einsum('bhcd,bhde->bhce', qc * jnp.exp(gc)[..., None], S)
             + jnp.einsum('bhij,bhje->bhie', qk, v_new))
        g_last = gc[..., -1:]
        S = (S * jnp.exp(g_last)[..., None]
             + jnp.einsum('bhcd,bhce->bhde', kc * jnp.exp(g_last - gc)[..., None], v_new))
        return S, o

    S, o = lax.scan(step, s0, (chunkify(q), chunkify(k), chunkify(v), chunkify(g), chunkify(beta)))
    return jnp.moveaxis(o, (0, 2), (1, 3)).reshape(B, T, H, dv), S

def deltanet_mixer(h_ctx, h_lat, w_in, conv_w, a_log, dt_bias, norm_g, w_out, need_ctx_out):
    def prep(h):
        B, T, _ = h.shape
        proj = h @ w_in
        qkv = jax.nn.silu(centred_dwconv(proj[..., :DN_CONV_W], conv_w))
        q = l2norm(qkv[..., :DN_KEY_W].reshape(B, T, DN_QK_HEADS, DN_HEAD_DIM))
        k = l2norm(qkv[..., DN_KEY_W:2 * DN_KEY_W].reshape(B, T, DN_QK_HEADS, DN_HEAD_DIM))
        v = qkv[..., 2 * DN_KEY_W:].reshape(B, T, DN_V_HEADS, DN_HEAD_DIM).astype(jnp.float32)
        q = jnp.repeat(q, DN_REP, axis=2) * (DN_HEAD_DIM ** -0.5)
        k = jnp.repeat(k, DN_REP, axis=2)
        z = proj[..., DN_CONV_W:DN_CONV_W + DN_VAL_W].reshape(B, T, DN_V_HEADS, DN_HEAD_DIM)
        gates = proj[..., DN_CONV_W + DN_VAL_W:].astype(jnp.float32).reshape(B, T, 2, 2, DN_V_HEADS)
        beta = jax.nn.sigmoid(gates[..., 0, :])
        g = -jnp.exp(a_log) * jax.nn.softplus(gates[..., 1, :] + dt_bias)
        return q, k, v, g, beta, z

    def bidir(q, k, v, g, beta, s_f, s_b):
        o_f, s_f = gated_delta_chunked(q, k, v, g[:, :, 0], beta[:, :, 0], s_f)
        fl = lambda a: jnp.flip(a, axis=1)
        o_b, s_b = gated_delta_chunked(fl(q), fl(k), fl(v), fl(g[:, :, 1]), fl(beta[:, :, 1]), s_b)
        return o_f + fl(o_b), s_f, s_b

    def out(o, z, dtype):
        B, T = o.shape[:2]
        o = rmsnorm(o, norm_g) * jax.nn.silu(z.astype(jnp.float32))
        return o.reshape(B, T, DN_VAL_W).astype(dtype) @ w_out

    qc, kc, vc, gc, bc, zc = prep(h_ctx)
    B = h_ctx.shape[0]
    s0 = jnp.zeros((B, DN_V_HEADS, DN_HEAD_DIM, DN_HEAD_DIM), jnp.float32)
    o_c, s_f, s_b = bidir(qc, kc, vc, gc, bc, s0, s0)
    ql, kl, vl, gl, bl, zl = prep(h_lat)
    o_l, _, _ = bidir(ql, kl, vl, gl, bl, s_f, s_b)
    y_c = out(o_c, zc, h_ctx.dtype) if need_ctx_out else None
    return y_c, out(o_l, zl, h_lat.dtype)

def gqa_attend(q, k, v):
    s = jnp.einsum('bqhgd,bkhd->bhgqk', q, k).astype(jnp.float32) * (ATT_HEAD_DIM ** -0.5)
    p = jax.nn.softmax(s, axis=-1).astype(v.dtype)
    return jnp.einsum('bhgqk,bkhd->bqhgd', p, v)

def attention_mixer(h_ctx, h_lat, w_in, qn_g, kn_g, w_out, cos, sin, need_ctx_out):
    def proj(h):
        B, T, _ = h.shape
        p = h @ w_in
        q = p[..., :ATT_Q_W].reshape(B, T, ATT_Q_HEADS, ATT_HEAD_DIM)
        k = rmsnorm(p[..., ATT_Q_W:ATT_Q_W + ATT_KV_W].reshape(B, T, ATT_KV_HEADS, ATT_HEAD_DIM), kn_g)
        v = p[..., ATT_Q_W + ATT_KV_W:].reshape(B, T, ATT_KV_HEADS, ATT_HEAD_DIM)
        return q, k, v

    q_c, k_c, v_c = proj(h_ctx)
    q_l, k_l, v_l = proj(h_lat)
    q_l = apply_rope(rmsnorm(q_l, qn_g), cos, sin)
    k_l = apply_rope(k_l, cos, sin)
    keys = jnp.concatenate([k_c, k_l], axis=1)
    vals = jnp.concatenate([v_c, v_l], axis=1)
    B, T = h_lat.shape[:2]
    nblk = T // ATT_BLOCK
    qb = q_l.reshape(B, nblk, ATT_BLOCK, ATT_KV_HEADS, ATT_GROUP, ATT_HEAD_DIM).swapaxes(0, 1)
    o_l = lax.map(lambda blk: gqa_attend(blk, keys, vals), qb)
    y_l = o_l.swapaxes(0, 1).reshape(B, T, ATT_Q_W) @ w_out
    y_c = None
    if need_ctx_out:
        Lc = h_ctx.shape[1]
        q_c = rmsnorm(q_c, qn_g).reshape(B, Lc, ATT_KV_HEADS, ATT_GROUP, ATT_HEAD_DIM)
        y_c = gqa_attend(q_c, k_c, v_c).reshape(B, Lc, ATT_Q_W) @ w_out
    return y_c, y_l

def peer(h, w_query, sub_keys, u_tab, v_tab):
    B, T, D = h.shape
    blocks = h.reshape(-1, PEER_TOKEN_BLOCK, D)

    def block_fn(xb):
        P = xb.shape[0]
        qry = (xb @ w_query).reshape(P, PEER_HEADS, 2, PEER_HALF)
        s = jnp.einsum('phcd,hckd->phck', qry, sub_keys).astype(jnp.float32)
        top_s, top_i = lax.top_k(s, PEER_TOPK)
        cand_s = (top_s[..., 0, :, None] + top_s[..., 1, None, :]).reshape(P, PEER_HEADS, PEER_TOPK * PEER_TOPK)
        cand_i = (top_i[..., 0, :, None] * PEER_N_KEYS + top_i[..., 1, None, :]).reshape(P, PEER_HEADS, PEER_TOPK * PEER_TOPK)
        best_s, pos = lax.top_k(cand_s, PEER_TOPK)
        idx = jnp.take_along_axis(cand_i, pos, axis=-1)
        gate = jax.nn.softmax(best_s, axis=-1)
        act = jax.nn.gelu(jnp.einsum('pd,phkd->phk', xb, u_tab[idx]).astype(jnp.float32), approximate=False)
        coef = (gate * act).astype(xb.dtype)
        return jnp.einsum('phk,phkd->pd', coef, v_tab[idx])

    return lax.map(block_fn, blocks).reshape(B, T, D)

def first_inputs(seed: int = 0) -> dict:
    key = jax.random.key(seed)
    ks = jax.random.split(key, 24)
    f32 = jnp.float32

    def nrm(k, shape, scale):
        return jax.random.normal(k, shape, f32) * scale

    def gain(k, shape):
        return 1.0 + 0.02 * jax.random.normal(k, shape, f32)

    dt = jnp.exp(jax.random.uniform(ks[13], (N_DN_LAYERS, 2, DN_V_HEADS), f32, math.log(1e-3), math.log(1e-1)))
    return {
        'x': nrm(ks[0], (BATCH, SEQ, D_MODEL), 1.0),
        'c': nrm(ks[1], (BATCH, D_MODEL), 1.0),
        'ctx': nrm(ks[2], (BATCH, CTX_LEN, D_MODEL), 1.0),
        'c_ctx': nrm(ks[3], (D_MODEL,), 1.0),
        'ada_w': nrm(ks[4], (DEPTH, D_MODEL, N_MOD * D_MODEL), 0.5 * D_MODEL ** -0.5),
        'ada_b': nrm(ks[5], (DEPTH, N_MOD * D_MODEL), 0.02),
        'norm1_g': gain(ks[6], (DEPTH, D_MODEL)),
        'norm2_g': gain(ks[7], (DEPTH, D_MODEL)),
        'final_g': gain(ks[8], (D_MODEL,)),
        'dn_w_in': nrm(ks[9], (N_DN_LAYERS, D_MODEL, DN_IN_W), D_MODEL ** -0.5),
        'dn_conv_w': nrm(ks[10], (N_DN_LAYERS, DN_CONV, DN_CONV_W), DN_CONV ** -0.5),
        'dn_a_log': jnp.log(jax.random.uniform(ks[11], (N_DN_LAYERS, 2, DN_V_HEADS), f32, 1.0, 16.0)),
        'dn_dt_bias': dt + jnp.log(-jnp.expm1(-dt)),
        'dn_norm_g': gain(ks[12], (N_DN_LAYERS, DN_HEAD_DIM)),
        'dn_w_out': nrm(ks[14], (N_DN_LAYERS, DN_VAL_W, D_MODEL), DN_VAL_W ** -0.5),
        'att_w_in': nrm(ks[15], (N_ATT_LAYERS, D_MODEL, ATT_IN_W), D_MODEL ** -0.5),
        'att_qn_g': gain(ks[16], (N_ATT_LAYERS, ATT_HEAD_DIM)),
        'att_kn_g': gain(ks[17], (N_ATT_LAYERS, ATT_HEAD_DIM)),
        'att_w_out': nrm(ks[18], (N_ATT_LAYERS, ATT_Q_W, D_MODEL), ATT_Q_W ** -0.5),
        'peer_w_query': nrm(ks[19], (DEPTH, D_MODEL, PEER_HEADS * PEER_QUERY_DIM), D_MODEL ** -0.5),
        'peer_sub_keys': nrm(ks[20], (DEPTH, PEER_HEADS, 2, PEER_N_KEYS, PEER_HALF), PEER_HALF ** -0.5),
        'peer_u': nrm(ks[21], (DEPTH, PEER_N_EXPERTS, D_MODEL), D_MODEL ** -0.5),
        'peer_v': nrm(ks[22], (DEPTH, PEER_N_EXPERTS, D_MODEL), PEER_HEADS ** -0.5),
    }

def first_block(x, c, ctx, c_ctx, ada_w, ada_b, norm1_g, norm2_g, final_g,
              dn_w_in, dn_conv_w, dn_a_log, dn_dt_bias, dn_norm_g, dn_w_out,
              att_w_in, att_qn_g, att_kn_g, att_w_out,
              peer_w_query, peer_sub_keys, peer_u, peer_v):
    cos, sin = axial_rope_tables(x.shape[1])
    cond_lat = jax.nn.silu(c)
    cond_ctx = jax.nn.silu(c_ctx)[None]
    xl, xc = x, ctx
    for i in range(DEPTH):
        last = i == DEPTH - 1
        sh1l, sc1l, g1l, sh2l, sc2l, g2l = ada_params(cond_lat, ada_w[i], ada_b[i])
        sh1c, sc1c, g1c, sh2c, sc2c, g2c = ada_params(cond_ctx, ada_w[i], ada_b[i])
        hl = rmsnorm(xl, norm1_g[i]) * (1.0 + sc1l) + sh1l
        hc = rmsnorm(xc, norm1_g[i]) * (1.0 + sc1c) + sh1c
        j = i // 2
        if i % 2 == 0:
            yc, yl = deltanet_mixer(hc, hl, dn_w_in[j], dn_conv_w[j], dn_a_log[j], dn_dt_bias[j],
                                    dn_norm_g[j], dn_w_out[j], not last)
        else:
            yc, yl = attention_mixer(hc, hl, att_w_in[j], att_qn_g[j], att_kn_g[j], att_w_out[j],
                                     cos, sin, not last)
        xl = xl + g1l * yl
        hl = rmsnorm(xl, norm2_g[i]) * (1.0 + sc2l) + sh2l
        xl = xl + g2l * peer(hl, peer_w_query[i], peer_sub_keys[i], peer_u[i], peer_v[i])
        if not last:
            xc = xc + g1c * yc
            hc = rmsnorm(xc, norm2_g[i]) * (1.0 + sc2c) + sh2c
            xc = xc + g2c * peer(hc, peer_w_query[i], peer_sub_keys[i], peer_u[i], peer_v[i])
    return rmsnorm(xl, final_g)


N_EVEN = (DEPTH + 1) // 2
N_ODD = DEPTH // 2
A_GROUPS = 4
A_CHUNK = 128
A_WIDTH = D_MODEL // 2
A_GROUP_CH = A_WIDTH // A_GROUPS
B_HEADS = 8
B_HEAD_DIM = 64
B_WIDTH = B_HEADS * B_HEAD_DIM
Q_BLOCK = 128
MIX_WIDTH = A_WIDTH + B_WIDTH
IN_COLS = 2 * A_WIDTH + 3 * B_WIDTH + B_HEADS
S5_GROUP_CH = 16
S5_GROUPS = D_MODEL // S5_GROUP_CH
S5_STATE = 64
D_FF = 2816
CONV_W = 3
PLE_DIM = 256
NEG_INF = -1e30


def rms_norm(x, g=None):
    xf = x.astype(jnp.float32)
    y = xf * lax.rsqrt(jnp.mean(xf * xf, axis=-1, keepdims=True) + EPS)
    if g is not None:
        y = y * g.astype(jnp.float32)
    return y.astype(x.dtype)

def gmlp_mixer(u, v, v_gain, w_s, b_s):
    bsz, seq = u.shape[0], u.shape[1]
    u = jax.nn.gelu(u)
    v = jax.nn.gelu(v).reshape(bsz, seq, A_GROUPS, A_GROUP_CH)
    v = rms_norm(v, v_gain.reshape(A_GROUPS, A_GROUP_CH))
    v = v.reshape(bsz, seq // A_CHUNK, A_CHUNK, A_GROUPS, A_GROUP_CH)
    tri = jnp.tril(jnp.ones((A_CHUNK, A_CHUNK), dtype=bool))
    w = jnp.where(tri[None], w_s, jnp.zeros_like(w_s))
    sv = jnp.einsum('gts,bnsgc->bntgc', w, v) + b_s.T[None, None, :, :, None]
    return u * sv.reshape(bsz, seq, A_WIDTH)

def fox_attention(q, k, v, f_logit, q_gain, k_gain):
    bsz, seq = q.shape[0], q.shape[1]
    q = rms_norm(q, q_gain)
    k = rms_norm(k, k_gain)
    c = jnp.cumsum(jax.nn.log_sigmoid(f_logit.astype(jnp.float32)), axis=1)
    nb = seq // Q_BLOCK
    qb = q.reshape(bsz, nb, Q_BLOCK, B_HEADS, B_HEAD_DIM).transpose(1, 0, 2, 3, 4)
    cb = c.reshape(bsz, nb, Q_BLOCK, B_HEADS).transpose(1, 0, 2, 3)
    pos_b = jnp.arange(seq, dtype=jnp.int32).reshape(nb, Q_BLOCK)
    kpos = jnp.arange(seq, dtype=jnp.int32)
    ck = c.transpose(0, 2, 1)
    scale = B_HEAD_DIM ** -0.5

    def block(args):
        qi, ci, pi = args
        s = jnp.einsum('bqhd,bkhd->bhqk', qi, k).astype(jnp.float32) * scale
        s = s + ci.transpose(0, 2, 1)[..., None] - ck[:, :, None, :]
        s = jnp.where(kpos[None, :] <= pi[:, None], s, NEG_INF)
        pr = jax.nn.softmax(s, axis=-1)
        return jnp.einsum('bhqk,bkhd->bqhd', pr.astype(v.dtype), v)

    o = lax.map(block, (qb, cb, pos_b))
    return o.transpose(1, 0, 2, 3, 4).reshape(bsz, seq, B_WIDTH)

def _complex_affine_combine(e1, e2):
    a1r, a1i, b1r, b1i = e1
    a2r, a2i, b2r, b2i = e2
    ar = a2r * a1r - a2i * a1i
    ai = a2r * a1i + a2i * a1r
    br = a2r * b1r - a2i * b1i + b2r
    bi = a2r * b1i + a2i * b1r + b2i
    return (ar, ai, br, bi)

def s5_mixer(u, a_re, a_im, log_dt, b_re, b_im, c_re, c_im, d):
    bsz, seq, _ = u.shape
    f32 = jnp.float32
    uf = u.astype(f32).reshape(bsz, seq, S5_GROUPS, S5_GROUP_CH)
    dt = jnp.exp(log_dt.astype(f32))[:, None]
    lr, li = a_re.astype(f32), a_im.astype(f32)
    mag = jnp.exp(lr * dt)
    ab_re, ab_im = mag * jnp.cos(li * dt), mag * jnp.sin(li * dt)
    den = lr * lr + li * li
    nr, ni = ab_re - 1.0, ab_im
    cr = (nr * lr + ni * li) / den
    ci = (ni * lr - nr * li) / den
    br, bi = b_re.astype(f32), b_im.astype(f32)
    bb_re = cr[..., None] * br - ci[..., None] * bi
    bb_im = cr[..., None] * bi + ci[..., None] * br
    bu_re = jnp.einsum('gpc,bsgc->bsgp', bb_re, uf)
    bu_im = jnp.einsum('gpc,bsgc->bsgp', bb_im, uf)
    a_r = jnp.broadcast_to(ab_re, bu_re.shape)
    a_i = jnp.broadcast_to(ab_im, bu_im.shape)
    _, _, xr, xi = lax.associative_scan(_complex_affine_combine, (a_r, a_i, bu_re, bu_im), axis=1)
    y = (jnp.einsum('gcp,bsgp->bsgc', c_re.astype(f32), xr)
         - jnp.einsum('gcp,bsgp->bsgc', c_im.astype(f32), xi)
         + d.astype(f32).reshape(S5_GROUPS, S5_GROUP_CH) * uf)
    return y.reshape(bsz, seq, D_MODEL).astype(u.dtype)

def conv_ffn(x, w_up, conv_w, conv_b, w_down):
    seq = x.shape[1]
    h = x @ w_up
    hp = jnp.pad(h, ((0, 0), (CONV_W - 1, 0), (0, 0)))
    hc = conv_b + conv_w[0] * hp[:, 0:seq]
    for j in range(1, CONV_W):
        hc = hc + conv_w[j] * hp[:, j:j + seq]
    g, up = jnp.split(hc, 2, axis=-1)
    return (jax.nn.silu(g) * up) @ w_down

def second_inputs(seed: int = 0) -> dict:
    key = jax.random.key(seed)
    ks = jax.random.split(key, 32)
    f32 = jnp.float32

    def nrm(k, shape, scale):
        return scale * jax.random.normal(k, shape, f32)

    a_im_base = jnp.broadcast_to(math.pi * jnp.arange(S5_STATE, dtype=f32), (N_ODD, S5_GROUPS, S5_STATE))
    return {
        "x": nrm(ks[0], (BATCH, SEQ, D_MODEL), 1.0),
        "p": nrm(ks[1], (DEPTH, BATCH, SEQ, PLE_DIM), 1.0),
        "norm_mix": 1.0 + nrm(ks[2], (DEPTH, D_MODEL), 0.05),
        "norm_ffn": 1.0 + nrm(ks[3], (DEPTH, D_MODEL), 0.05),
        "ev_w_in": nrm(ks[4], (N_EVEN, D_MODEL, IN_COLS), D_MODEL ** -0.5),
        "ev_b_fgate": 4.0 + nrm(ks[5], (N_EVEN, B_HEADS), 0.5),
        "ev_q_norm": 1.0 + nrm(ks[6], (N_EVEN, B_HEAD_DIM), 0.05),
        "ev_k_norm": 1.0 + nrm(ks[7], (N_EVEN, B_HEAD_DIM), 0.05),
        "ev_v_norm": 1.0 + nrm(ks[8], (N_EVEN, A_WIDTH), 0.05),
        "ev_w_spatial": nrm(ks[9], (N_EVEN, A_GROUPS, A_CHUNK, A_CHUNK), A_CHUNK ** -0.5),
        "ev_b_spatial": 1.0 + nrm(ks[10], (N_EVEN, A_GROUPS, A_CHUNK), 0.1),
        "ev_w_out": nrm(ks[11], (N_EVEN, MIX_WIDTH, D_MODEL), MIX_WIDTH ** -0.5),
        "od_a_re": -0.5 + nrm(ks[12], (N_ODD, S5_GROUPS, S5_STATE), 0.01),
        "od_a_im": a_im_base + nrm(ks[13], (N_ODD, S5_GROUPS, S5_STATE), 0.01),
        "od_log_dt": jax.random.uniform(ks[14], (N_ODD, S5_GROUPS), f32, math.log(1e-3), math.log(1e-1)),
        "od_b_re": nrm(ks[15], (N_ODD, S5_GROUPS, S5_STATE, S5_GROUP_CH), (2 * S5_GROUP_CH) ** -0.5),
        "od_b_im": nrm(ks[16], (N_ODD, S5_GROUPS, S5_STATE, S5_GROUP_CH), (2 * S5_GROUP_CH) ** -0.5),
        "od_c_re": nrm(ks[17], (N_ODD, S5_GROUPS, S5_GROUP_CH, S5_STATE), S5_STATE ** -0.5),
        "od_c_im": nrm(ks[18], (N_ODD, S5_GROUPS, S5_GROUP_CH, S5_STATE), S5_STATE ** -0.5),
        "od_d": nrm(ks[19], (N_ODD, D_MODEL), 1.0),
        "od_w_glu": nrm(ks[20], (N_ODD, D_MODEL, 2 * D_MODEL), D_MODEL ** -0.5),
        "ffn_w_up": nrm(ks[21], (DEPTH, D_MODEL, 2 * D_FF), D_MODEL ** -0.5),
        "ffn_conv_w": nrm(ks[22], (DEPTH, CONV_W, 2 * D_FF), CONV_W ** -0.5),
        "ffn_conv_b": nrm(ks[23], (DEPTH, 2 * D_FF), 0.02),
        "ffn_w_down": nrm(ks[24], (DEPTH, D_FF, D_MODEL), D_FF ** -0.5),
        "ple_w_proj": nrm(ks[25], (DEPTH, PLE_DIM, D_MODEL), PLE_DIM ** -0.5),
        "ple_w_gate": nrm(ks[26], (DEPTH, D_MODEL, D_MODEL), D_MODEL ** -0.5),
    }

def second_block(x, p, norm_mix, norm_ffn, ev_w_in, ev_b_fgate, ev_q_norm, ev_k_norm, ev_v_norm,
              ev_w_spatial, ev_b_spatial, ev_w_out, od_a_re, od_a_im, od_log_dt, od_b_re, od_b_im,
              od_c_re, od_c_im, od_d, od_w_glu, ffn_w_up, ffn_conv_w, ffn_conv_b, ffn_w_down,
              ple_w_proj, ple_w_gate):
    bsz, seq = x.shape[0], x.shape[1]
    splits = [A_WIDTH, 2 * A_WIDTH, 2 * A_WIDTH + B_WIDTH, 2 * A_WIDTH + 2 * B_WIDTH,
              2 * A_WIDTH + 3 * B_WIDTH]
    for i in range(DEPTH):
        h = rms_norm(x, norm_mix[i])
        if i % 2 == 0:
            e = i // 2
            z = h @ ev_w_in[e]
            u_a, v_a, q, k, v_b, f = jnp.split(z, splits, axis=-1)
            y_a = gmlp_mixer(u_a, v_a, ev_v_norm[e], ev_w_spatial[e], ev_b_spatial[e])
            shp = (bsz, seq, B_HEADS, B_HEAD_DIM)
            y_b = fox_attention(q.reshape(shp), k.reshape(shp), v_b.reshape(shp),
                                f + ev_b_fgate[e], ev_q_norm[e], ev_k_norm[e])
            x = x + jnp.concatenate([y_a, y_b], axis=-1) @ ev_w_out[e]
        else:
            o = i // 2
            y = s5_mixer(h, od_a_re[o], od_a_im[o], od_log_dt[o], od_b_re[o], od_b_im[o],
                         od_c_re[o], od_c_im[o], od_d[o])
            g_a, g_b = jnp.split(jax.nn.gelu(y) @ od_w_glu[o], 2, axis=-1)
            x = x + g_a * jax.nn.sigmoid(g_b)
        x = x + conv_ffn(rms_norm(x, norm_ffn[i]), ffn_w_up[i], ffn_conv_w[i], ffn_conv_b[i], ffn_w_down[i])
        gate = jax.nn.sigmoid(rms_norm(x) @ ple_w_gate[i])
        x = x + gate * (p[i] @ ple_w_proj[i])
    return x


def setup_inputs(seed=0):
    out = dict(first_inputs(seed))
    for name, value in second_inputs(seed + 1).items():
        if name != "x":
            out[name + "_2"] = value
    return out


def reference(
    x, c, ctx, c_ctx, ada_w, ada_b, norm1_g, norm2_g, final_g, dn_w_in, dn_conv_w, dn_a_log,
    dn_dt_bias, dn_norm_g, dn_w_out, att_w_in, att_qn_g, att_kn_g, att_w_out, peer_w_query,
    peer_sub_keys, peer_u, peer_v, p_2, norm_mix_2, norm_ffn_2, ev_w_in_2, ev_b_fgate_2,
    ev_q_norm_2, ev_k_norm_2, ev_v_norm_2, ev_w_spatial_2, ev_b_spatial_2, ev_w_out_2,
    od_a_re_2, od_a_im_2, od_log_dt_2, od_b_re_2, od_b_im_2, od_c_re_2, od_c_im_2, od_d_2,
    od_w_glu_2, ffn_w_up_2, ffn_conv_w_2, ffn_conv_b_2, ffn_w_down_2, ple_w_proj_2,
    ple_w_gate_2,
):
    x = first_block(
        x, c, ctx, c_ctx, ada_w, ada_b, norm1_g, norm2_g, final_g, dn_w_in, dn_conv_w, dn_a_log,
        dn_dt_bias, dn_norm_g, dn_w_out, att_w_in, att_qn_g, att_kn_g, att_w_out, peer_w_query,
        peer_sub_keys, peer_u, peer_v,
    )
    return second_block(
        x, p_2, norm_mix_2, norm_ffn_2, ev_w_in_2, ev_b_fgate_2, ev_q_norm_2, ev_k_norm_2,
        ev_v_norm_2, ev_w_spatial_2, ev_b_spatial_2, ev_w_out_2, od_a_re_2, od_a_im_2,
        od_log_dt_2, od_b_re_2, od_b_im_2, od_c_re_2, od_c_im_2, od_d_2, od_w_glu_2, ffn_w_up_2,
        ffn_conv_w_2, ffn_conv_b_2, ffn_w_down_2, ple_w_proj_2, ple_w_gate_2,
    )


_drawn_inputs = setup_inputs


def setup_inputs(seed=0):
    import zlib

    import numpy as np

    out = dict(_drawn_inputs(seed))
    spreads = {}
    factors = {'norm1_g': 5.161,
     'norm2_g': 4.017,
     'dn_norm_g': 6.973,
     'att_qn_g': 8.0,
     'att_kn_g': 8.0,
     'ev_q_norm_2': 8.0,
     'ev_k_norm_2': 8.0,
     'ev_v_norm_2': 3.838,
     'od_a_re_2': 64.0,
     'od_a_im_2': 18.418,
     'od_log_dt_2': 20.508,
     'od_b_re_2': 31.416,
     'od_b_im_2': 30.04,
     'od_c_re_2': 31.424,
     'od_c_im_2': 31.088,
     'ffn_conv_b_2': 3.439}
    for name, (base, spread) in spreads.items():
        noise = np.random.default_rng([zlib.crc32(name.encode()), seed]).standard_normal(out[name].shape)
        drawn = base * np.exp(spread * noise) if base else spread * noise
        out[name] = jnp.asarray(drawn.astype(out[name].dtype))
    for name, factor in factors.items():
        out[name] = (out[name] * factor).astype(out[name].dtype)
    return out
```

```python
from contextlib import ExitStack

import numpy as np

import concourse.bass as bass
import concourse.mybir as mybir

F32 = mybir.dt.float32
BF16 = mybir.dt.bfloat16
U32 = mybir.dt.uint32
ALU = mybir.AluOpType
ACT = mybir.ActivationFunctionType
AX = mybir.AxisListType.X

SPAN = 4000


class Engine:

    def __init__(self, name, new_sem):
        self.name, self.new_sem = name, new_sem
        self.items, self.nsem, self.made = [], 0, {}
        self.last = None

    def wait(self, *marks):
        for m in marks:
            if isinstance(m, list):
                self.wait(*m)
            elif m is not None and self.made.get(m[0], 0) < m[1]:
                self.made[m[0]] = m[1]
                self.items.append(("wait", m[0], m[1]))

    def count(self, at=-1):
        if self.last is None or self.last[1] == SPAN:
            self.last = (self.new_sem(f"s_{self.name}{self.nsem}"), 0)
            self.nsem += 1
        self.last = (self.last[0], self.last[1] + 1)
        self.items[at] = ("inc", self.items[at][1], self.last[0], 1)
        return self.last

    def dma(self, lane, out, in_):
        lane.n += 16
        self.items.append(("inc", lambda e: e.dma_start(out, in_), lane.sem, 16))
        return lane.sem, lane.n

    def emit(self, eng):
        for item in self.items:
            if item[0] == "wait":
                eng.wait_ge(item[1], item[2])
            elif item[0] == "inc":
                item[1](eng).then_inc(item[2], item[3])
            else:
                item[1](eng)


class Tensor(Engine):

    def do(self, fn):
        self.at, self.counted = len(self.items), False
        self.items.append(("do", fn))

    def done(self):
        if not self.counted:
            self.counted = True
            self.count(self.at)
        return self.last

    def mm(self, out, l, r, start, stop, at=None):
        if at is None:
            self.do(lambda e: e.matmul(out, l, r, start=start, stop=stop))
        else:
            self.do(lambda e: e.matmul(out, l, r, start=start, stop=stop, tile_position=at))

    def tr(self, out, in_):
        n = in_.shape[0]
        self.do(lambda e: e.transpose(out, in_, self.ident[0:n, 0:n]))


class Lanes(Engine):

    def do(self, fn):
        if self.last is not None:
            self.wait(self.last)
        self.items.append(("do", fn))
        return self.count()

    def cp(self, out, in_):
        return self.do(lambda e: e.tensor_copy(out, in_))

    def tt(self, out, a, b, op):
        return self.do(lambda e: e.tensor_tensor(out, a, b, op))

    def ts(self, out, a, s1, s2, op0, op1):
        if s2 is None:
            return self.do(lambda e: e.tensor_scalar(out, a, s1, None, op0))
        return self.do(lambda e: e.tensor_scalar(out, a, s1, s2, op0, op1))

    def stt(self, out, a, s, b, op0, op1):
        return self.do(lambda e: e.scalar_tensor_tensor(out, a, s, b, op0, op1))

    def red(self, out, in_, op):
        return self.do(lambda e: e.tensor_reduce(out, in_, AX, op))

    def rec(self, out, in_):
        return self.do(lambda e: e.reciprocal(out, in_))

    def ms(self, out, v):
        return self.do(lambda e: e.memset(out, v))

    def scan(self, out, d0, d1):
        return self.do(lambda e: e.tensor_tensor_scan(out, d0, d1, 0.0, ALU.mult, ALU.add))


class Scalar(Lanes):
    def ac(self, out, in_, f, bias=0.0, scale=1.0, acc=None):
        return self.do(lambda e: e.activation(out, in_, f, bias=bias, scale=scale, accum_out=acc))

    def cp(self, out, in_):
        return self.ac(out, in_, ACT.Copy)


class Lane:

    def __init__(self, sem):
        self.sem, self.n = sem, 0


class Bank:

    def __init__(self, ap):
        self.ap, self.free = ap, []


class Slot:

    def __init__(self, ap, lane):
        self.ap, self.lane, self.free, self.tok = ap, lane, [], None


LEVELS = [1, 2, 4, 8, 16, 32, 64]
TILES = 4
NEG = -1.0e30


def constants():
    i = np.arange(128)
    r, c = i[:, None], i[None, :]
    parts = {
        "ident": r == c, "le": r <= c, "gt": r > c, "ge": r >= c, "lt": r < c,
        "ones": np.ones((128, 128)), "iota": np.broadcast_to(c, (128, 128)),
        "par": np.stack([(i // 16) % 2 == 0, (i // 16) % 2 == 1, i < 64, i >= 64], 1),
        "sel": np.stack([np.broadcast_to(i == h, (128, 128)).T for h in range(8)], 1).reshape(128, 1024),
    }
    t = np.arange(256)
    parts["causal"] = np.concatenate([np.where(t[None, :] <= 128 * n + r, 0.0, NEG) for n in range(2)], 1)
    inv = 10000.0 ** (-np.arange(0, 64, 2, dtype=np.float32) / np.float32(64))
    ang = np.concatenate([(t // 64)[:, None] * inv, (t % 64)[:, None] * inv], 1).astype(np.float32)
    for name, f in (("cos", np.cos), ("sin", np.sin)):
        parts[name] = f(ang).reshape(2, 128, 64).transpose(1, 0, 2).reshape(128, 128)
    lev = []
    for s in LEVELS:
        m = (r // (2 * s) == c // (2 * s)) & ((r // s) % 2 == 1) & ((c // s) % 2 == 0)
        lev += [m, m.T]
    parts["lev"] = np.concatenate(lev, 1)
    off, at = {}, 0
    for k, v in parts.items():
        off[k] = (at, v.shape[1])
        at += v.shape[1]
    return np.concatenate([np.asarray(v, np.float32) for v in parts.values()], 1), off


VECS = [("norm1_g", 0), ("norm1_g", 1), ("norm2_g", 0), ("norm2_g", 1), ("norm_mix_2", 0), ("norm_mix_2", 1),
        ("norm_ffn_2", 0), ("norm_ffn_2", 1), ("od_d_2", 0), ("c", 0), ("c_ctx", None)]


class Model:
    def __init__(self, nc, ins, out, ctx):
        self.nc, self.i, self.out, self.ctx = nc, ins, out, ctx
        self.nsem = 0
        self.P = Tensor("pe", self.sem)
        self.V = Lanes("dve", self.sem)
        self.S = Scalar("act", self.sem)
        self.G = Lanes("pool", self.sem)
        self.SP = Engine("sp", self.sem)
        self.psum = ctx.enter_context(nc.psum_tensor("psum", [128, 8, 512], F32))
        self.banks = [Bank(self.psum[:, b, :]) for b in range(8)]
        self.X = self.tensor("x_res", 4 * 1024).rearrange("p (t d) -> p t d", t=4)
        self.ring = [Slot(self.tensor(f"ring{n}", 2048), Lane(self.sem(f"l_ring{n}"))) for n in range(3)]
        self.nring = 0
        self.cv, self.off = None, None
        self.mod = self.tensor("mod", 2 * 4 * 8 * 2).rearrange("p (l k c v) -> p l k c v", l=2, k=4, c=8)
        self.vc = self.tensor("vc", 128)
        self.small = self.tensor("small", 64)
        self.arena_n = 41500
        self.arena = self.tensor("arena", self.arena_n)
        self.top = 0
        self.flip = 0
        self.stores = []

    def sem(self, name):
        self.nsem += 1
        return self.ctx.enter_context(self.nc.semaphore(name))

    def tensor(self, name, n, dt=F32):
        return self.ctx.enter_context(self.nc.sbuf_tensor(name, [128, n], dt))[:, :]

    def al(self, n, shape=None, names=None):
        a = self.arena[:, self.top:self.top + n]
        self.top += n
        assert self.top <= self.arena_n, self.top
        return a

    def al2(self, a, b):
        return self.al(a * b).rearrange("p (a b) -> p a b", a=a)

    def al3(self, a, b, c):
        return self.al(a * b * c).rearrange("p (a b c) -> p a b c", a=a, b=b)

    def stage(self):
        engines = [self.P, self.V, self.S, self.G]
        ends = [self.P.done(), self.V.last, self.S.last, self.G.last]
        for e in engines:
            e.wait(ends, self.stores)
        self.stores = []
        self.top = 0

    def const(self, name, a=0, n=None):
        o, w = self.off[name]
        return self.cv[:, o + a:o + (w if n is None else a + n)]

    def either(self):
        self.flip ^= 1
        return self.V if self.flip else self.S

    def misc(self, out, in_):
        return self.G.dma(Lane(self.sem(f"l_m{self.nsem}")), out, in_)

    def load(self, pieces):
        s = self.ring[self.nring % len(self.ring)]
        self.nring += 1
        self.SP.wait(s.free)
        for dst, src in pieces:
            s.tok = self.SP.dma(s.lane, dst(s.ap), src)
        s.free = None
        return s

    def rstd(self, out, ss, n, ready):
        self.V.wait(ready)
        t = self.V.ts(out, ss, 1.0 / n, 1e-06, ALU.mult, ALU.add)
        self.S.wait(t)
        t = self.S.ac(out, out, ACT.Sqrt)
        self.V.wait(t)
        return self.V.rec(out, out)

    def wslot(self, W, k0, nk, n0, nw):
        src = W[k0 * 128:(k0 + nk) * 128, n0:n0 + nw].rearrange("(k p) n -> p k n", p=128)
        s = self.load([(lambda a: a[:, 0:nk * nw].rearrange("p (k n) -> p k n", k=nk), src)])
        return s, s.ap[:, 0:nk * nw].rearrange("p (k n) -> p k n", k=nk)

    def proj_tok(self, hT, KC, W, N, ntile, cb, dep, banks=None, base=0):
        banks = banks or self.banks
        turn = 0
        self.P.wait(dep)
        for n0 in range(0, N, 512):
            nw = min(512, N - n0)
            bs = [banks[(turn + t) % len(banks)] for t in range(ntile)]
            turn += ntile
            for k0 in range(0, KC, 4):
                nk = min(4, KC - k0)
                s, w = self.wslot(W, k0, nk, base + n0, nw)
                self.P.wait(s.tok)
                for t in range(ntile):
                    self.P.wait(bs[t].free)
                    for k in range(nk):
                        self.P.mm(bs[t].ap[:, 0:nw], hT[:, k0 + k, t * 128:(t + 1) * 128], w[:, k, :], k0 + k == 0,
                                  k0 + k == KC - 1)
                    tk = self.P.done()
                    bs[t].done = tk
                s.free = [tk]
            for t in range(ntile):
                bs[t].free = [cb(t, n0, nw, bs[t].ap, bs[t].done)]

    def proj_feat(self, hT, KC, W, N, nt, cb, dep, banks=None, base=0):
        banks = banks or self.banks
        self.P.wait(dep)
        for n0 in range(0, N, 256):
            s, w = self.wslot(W, 0, KC, base + n0, 256)
            self.P.wait(s.tok)
            for j in range(2):
                b = banks[(n0 // 128 + j) % len(banks)]
                self.P.wait(b.free)
                for k in range(KC):
                    self.P.mm(b.ap[:, 0:nt], w[:, k, j * 128:(j + 1) * 128], hT[:, k, 0:nt], k == 0, k == KC - 1)
                tk = self.P.done()
                s.free = [tk]
                b.free = [cb(n0 // 128 + j, b.ap, tk)]

    def norm_T(self, tiles, hT, A, B, scr, dep=None, banks=None):
        banks = banks or self.banks[0:4]
        sq, st = scr[:, 0:1024], scr[:, 2048:2056]
        last = [None, None]
        self.S.wait(dep)
        for n, t in enumerate(tiles):
            a, b = A[n], B[n] if B is not None else None
            xn = scr[:, 1024:2048] if n % 2 == 0 else scr[:, 2056:3080]
            z = self.S.ac(sq, self.X[:, t, :], ACT.Square, acc=st[:, n:n + 1])
            z = self.rstd(st[:, n:n + 1], st[:, n:n + 1], 1024, z)
            free = self.xn_free[n % 2] if n >= 2 else None
            self.V.wait(z, free)
            z = self.V.ts(xn, self.X[:, t, :], st[:, n:n + 1], None, ALU.mult, None)
            self.P.wait(z)
            for half in range(2):
                bk = banks[(2 * n + half) % len(banks)]
                self.P.wait(bk.free)
                for k in range(4):
                    self.P.tr(bk.ap[:, k * 128:(k + 1) * 128], xn[:, (half * 4 + k) * 128:(half * 4 + k + 1) * 128])
                tk = self.P.done()
                for k in range(4):
                    c = half * 4 + k
                    o, i = hT[:, c, n * 128:(n + 1) * 128], bk.ap[:, k * 128:(k + 1) * 128]
                    if half == 0:
                        self.S.wait(tk)
                        f = self.S.ac(o, i, ACT.Identity, scale=a[:, c:c + 1], bias=b[:, c:c + 1] if b is not None else 0.0)
                    elif b is not None:
                        self.V.wait(tk)
                        f = self.V.ts(o, i, a[:, c:c + 1], b[:, c:c + 1], ALU.mult, ALU.add)
                    else:
                        self.V.wait(tk)
                        f = self.V.ts(o, i, a[:, c:c + 1], None, ALU.mult, None)
                bk.free = [f]
                last[half] = f
            self.xn_free[n % 2] = tk
        return last

    def to_T(self, src, n, dst, dep, banks=None):
        banks = banks or self.banks[0:4]
        toks = []
        self.P.wait(dep)
        for c0 in range(0, n, 4):
            m = min(4, n - c0)
            bk = banks[(c0 // 4) % len(banks)]
            self.P.wait(bk.free)
            for k in range(m):
                self.P.tr(bk.ap[:, k * 128:(k + 1) * 128], src[:, (c0 + k) * 128:(c0 + k + 1) * 128])
            tk = self.P.done()
            q = self.either()
            q.wait(tk)
            f = q.cp(dst[:, c0:c0 + m, :], bk.ap[:, 0:m * 128].rearrange("p (k n) -> p k n", k=m))
            bk.free = [f]
            toks.append(f)
        return toks[-2:]

    def begin(self):
        self.xn_free = [None, None]
        consts, self.off = constants()
        self.nconst = self.off["par"][0] + 4
        self.cv = self.tensor("consts", self.nconst)
        c_d = self.i["consts"]
        t = self.misc(self.cv, c_d[:, 0:self.nconst])
        self.ident = self.P.ident = self.const("ident")
        self.V.wait(t)
        z = self.V.ms(self.small, 0.0)
        for n, (name, d) in enumerate((("ctx", 0), ("x", 2))):
            self.xtok = self.misc(self.X[:, d:d + 2, :], self.i[name][0].rearrange("(t p) d -> p t d", p=128))
            self.V.wait(self.xtok)
            self.small_t = self.V.cp(self.small[:, n:n + 1], self.X[:, d, 0:1])
        rows = self.al(128)
        lane = Lane(self.sem("l_vec"))
        for n, (name, l) in enumerate(VECS):
            src = self.i[name] if l is None else self.i[name][l]
            t = self.G.dma(lane, rows[8 * n:8 * n + 8, :], src.rearrange("(k p) -> k p", p=128))
        t = self.G.dma(lane, rows[88:89, :], self.i["dn_norm_g"])
        t = self.G.dma(lane, rows[89:93, :], self.i["ev_b_spatial_2"][0])
        b = self.banks[0]
        self.P.wait(t, z, b.free)
        self.P.tr(b.ap[:, 0:93], rows[0:93, :])
        tk = self.P.done()
        self.V.wait(tk)
        self.vtok = self.V.cp(self.vc[:, 0:93], b.ap[:, 0:93])
        b.free = [self.vtok]
        self.P.wait(self.vtok, self.xtok)
        self.S.wait(self.vtok)
        self.G.wait(self.vtok)

    def vec(self, name, l):
        n = 8 * VECS.index((name, l))
        return self.vc[:, n:n + 8]

    def ada(self):
        self.stage()
        cond = self.al2(8, 2)
        t = None
        for v, name in enumerate((("c", 0), ("c_ctx", None))):
            t = self.S.ac(cond[:, :, v], self.vec(*name), ACT.Silu)
        rows = [self.al(6144), self.al(6144)]
        bias = [self.al(6144), self.al(6144)]
        self.gates_d = self.nc.dram_tensor("gates_d", [2, 2, 2, 1024], F32, kind="Internal").ap()
        self.gtok = {}
        self.P.wait(t)
        for l in range(2):
            bt = self.misc(bias[l][0:2, :], self.i["ada_b"][l].partition_broadcast(2))
            last = None
            self.V.wait(bt)
            for n in range(12):
                b = self.banks[n % 4]
                self.P.wait(b.free)
                for k0 in (0, 4):
                    s, w = self.wslot(self.i["ada_w"][l], k0, 4, n * 512, 512)
                    self.P.wait(s.tok)
                    for k in range(4):
                        self.P.mm(b.ap[0:2, :], cond[:, k0 + k, :], w[:, k, :], k0 + k == 0, k0 + k == 7)
                    tk = self.P.done()
                    s.free = [tk]
                self.V.wait(tk)
                last = self.V.tt(rows[l][0:2, n * 512:(n + 1) * 512], b.ap[0:2, :], bias[l][0:2, n * 512:(n + 1) * 512],
                                 ALU.add)
                b.free = [last]
            self.G.wait(last)
            for w_, o in enumerate((2048, 5120)):
                self.gtok[l, w_] = self.misc(self.gates_d[l, w_], rows[l][0:2, o:o + 1024])
                self.stores.append(self.gtok[l, w_])
            b = self.banks[4 + l]
            self.P.wait(last, b.free)
            for kind, o in enumerate((0, 1024, 3072, 4096)):
                for c in range(8):
                    q = (kind * 8 + c) * 2
                    self.P.tr(b.ap[:, q:q + 2], rows[l][0:2, o + c * 128:o + (c + 1) * 128])
            tk = self.P.done()
            m = self.mod[:, l]
            self.V.wait(tk)
            z = self.V.cp(m, b.ap[:, 0:64].rearrange("p (k c v) -> p k c v", k=4, c=8))
            b.free = [z]
            for kind, name in ((1, "norm1_g"), (3, "norm2_g")):
                for v in range(2):
                    self.mtok = self.V.stt(m[:, kind, :, v], m[:, kind, :, v], 1.0, self.vec(name, l), ALU.add, ALU.mult)
        for q in (self.S, self.P, self.G):
            q.wait(self.mtok)

    def gate_rows(self, l, which, v, place, ready=None):
        self.G.wait(self.gtok[l, which], ready)
        return (place, self.misc(place, self.gates_d[l, which, v].partition_broadcast(128)))

    def mod_cols(self, l, which, tiles):
        vs = [1 if t < 2 else 0 for t in tiles]
        return ([self.mod[:, l, 2 * which + 1, :, v] for v in vs], [self.mod[:, l, 2 * which, :, v] for v in vs])

    def add_gated(self, l, which, t, n0, nw, bank, tk, scr, gate):
        rows, got = gate[t // 2 if len(gate) > 1 else 0]
        self.V.wait(tk, got)
        z = self.V.tt(scr[:, 0:nw], bank[:, 0:nw], rows[:, n0:n0 + nw], ALU.mult)
        x = self.X[:, t, n0:n0 + nw]
        self.V.wait(z)
        self.V.tt(x, x, scr[:, 0:nw], ALU.add)
        return z

    def deltanet(self):
        self.stage()
        nc = self.nc
        W = self.i["dn_w_in"][0]
        hT = self.al2(8, 512)
        qT, kT, kt = self.al2(4, 512), self.al2(4, 512), self.al3(4, 4, 128)
        vt = self.al3(4, 8, 128)
        O = self.al3(4, 8, 128)
        lev = self.al(14 * 64).bitcast(BF16).rearrange("p (l m) -> p l m", l=14)
        cw = self.al2(32, 5)
        al, be, g = (self.al3(4, 2, 16) for _ in range(3))
        egc, erl, beg, egl = (self.al3(4, 2, 16) for _ in range(4))
        gates = self.al3(4, 2, 32)
        ssq, ssk = self.al2(4, 4), self.al2(4, 4)
        work = self.top
        scr = self.al(3080)
        A, B = self.mod_cols(0, 0, range(4))
        ht = self.norm_T(range(4), hT, A, B, scr)
        o = self.off["lev"][0]
        self.top = work + 3080
        tmp = self.al(14 * 128)
        t = self.misc(tmp, self.i["consts"][:, o:o + 14 * 128])
        self.V.wait(t)
        self.V.cp(lev, tmp.rearrange("p (l m) -> p l m", l=14))
        cr = self.al(4096)
        t = self.misc(cr[0:5, :], self.i["dn_conv_w"][0])
        b = self.banks[7]
        self.P.wait(t, b.free)
        for c in range(32):
            self.P.tr(b.ap[:, c * 5:c * 5 + 5], cr[0:5, c * 128:(c + 1) * 128])
        tk = self.P.done()
        self.V.wait(tk)
        z = self.V.cp(cw, b.ap[:, 0:160].rearrange("p (a b) -> p a b", a=32))
        b.free = [z]
        def gate_cols(t, n0, nw, bank, tk):
            self.V.wait(tk)
            return self.V.cp(gates[:, t], bank[:, 0:64].rearrange("p (d x) -> p d x", d=2))

        self.proj_tok(hT, 8, W, 64, 4, gate_cols, ht, base=6144)
        rows = self.al2(2, 32)
        lane = Lane(self.sem("l_alog"))
        self.G.dma(lane, rows[:, 0, :], self.i["dn_a_log"][0].rearrange("a b -> (a b)").partition_broadcast(128))
        t = self.G.dma(lane, rows[:, 1, :], self.i["dn_dt_bias"][0].rearrange("a b -> (a b)").partition_broadcast(128))
        r4 = [rows[:, n, :].rearrange("p (d h) -> p d h", d=2) for n in range(2)]
        self.S.wait(t)
        z = self.S.ac(rows[:, 0, :], rows[:, 0, :], ACT.Exp)
        sp = self.al3(4, 2, 16)
        for n in range(4):
            self.V.wait(z)
            z = self.V.tt(g[:, n], gates[:, n, :, 16:32], r4[1], ALU.add)
        self.S.wait(z)
        z = self.S.ac(sp, g, ACT.Abs)
        z = self.S.ac(sp, sp, ACT.Exp, scale=-1.0)
        self.V.wait(z)
        z = self.V.ts(sp, sp, 1.0, None, ALU.add, None)
        self.S.wait(z)
        z = self.S.ac(sp, sp, ACT.Ln)
        self.V.wait(z)
        z = self.V.stt(g, g, 0.0, sp, ALU.max, ALU.add)
        for n in range(4):
            self.V.wait(z)
            z = self.V.stt(g[:, n], g[:, n], -1.0, r4[0], ALU.mult, ALU.mult)
        self.S.wait(z)
        for n in range(4):
            bt = self.S.ac(be[:, n], gates[:, n, :, 0:16], ACT.Sigmoid)
        b = self.banks[6]
        self.P.wait(z, b.free)
        for n in range(4):
            for d in range(2):
                r = g[:, n, d, :]
                for w, m in enumerate((("le", "ge")[d], ("gt", "lt")[d], "ones")):
                    q = ((n * 2 + d) * 3 + w) * 16
                    self.P.mm(b.ap[:, q:q + 16], self.const(m), r, True, True)
        tk = self.P.done()
        bv = b.ap[:, 0:384].rearrange("p (n d w h) -> p n d w h", n=4, d=2, w=3)
        self.S.wait(tk)
        for n in range(4):
            for w, dst in enumerate((egc, erl, egl)):
                z = self.S.ac(dst[:, n], bv[:, n, :, w, :], ACT.Exp)
        b.free = [z]
        self.V.wait(z, bt)
        gt_ = self.V.tt(beg, be, egc, ALU.mult)
        gs = None
        self.P.wait(ht)
        for half in range(2):
            self.stage()
            self.top = work
            scr = self.al(512)
            pads = [self.al(520).rearrange("p (s t) -> p s t", s=2) for _ in range(2)]
            cvs = [self.al(512) for _ in range(2)]
            sqs = self.al(128)
            for p in pads:
                z = self.V.ms(p, 0.0)
            pfree, cfree = [z, z], [None, None]
            kb = self.banks[4:8]

            def conv(j, c, bank, tk):
                p, cv_ = pads[j % 2], cvs[j % 2]
                self.S.wait(tk, pfree[j % 2])
                z = self.S.ac(p[:, :, 2:258], bank.rearrange("p (s t) -> p s t", s=2), ACT.Copy)
                evac = z
                acc = cv_.rearrange("p (s t) -> p s t", s=2)
                self.V.wait(z, cfree[j % 2])
                z = self.V.ts(acc, p[:, :, 0:256], cw[:, c, 0:1], None, ALU.mult, None)
                for w in range(1, 5):
                    z = self.V.stt(acc, p[:, :, w:w + 256], cw[:, c, w:w + 1], acc, ALU.mult, ALU.add)
                pfree[j % 2] = z
                return evac, z, cv_

            def transposed(src, z, b):
                self.P.wait(z, b.free)
                for n in range(4):
                    self.P.tr(b.ap[:, n * 128:(n + 1) * 128], src[:, n * 128:(n + 1) * 128])
                tk = self.P.done()
                return tk

            jobs = [("q", half * 4 + n, n) for n in range(4)] + [("k", 8 + half * 4 + n, n) for n in range(4)] + \
                   [("v", 16 + half * 8 + n, n) for n in range(8)]
            for j0 in range(0, 16, 2):
                kind, c0, n0 = jobs[j0]
                s, w = self.wslot(W, 0, 8, c0 * 128, 256)
                self.P.wait(s.tok)
                for jj in range(2):
                    j = j0 + jj
                    kind, c, n = jobs[j]
                    b = self.banks[j % 4]
                    self.P.wait(b.free)
                    for k in range(8):
                        self.P.mm(b.ap, w[:, k, jj * 128:(jj + 1) * 128], hT[:, k, :], k == 0, k == 7)
                    tk = self.P.done()
                    s.free = [tk]
                    evac, z, cv_ = conv(j, c, b.ap, tk)
                    b.free = [evac]
                    tb = kb[j % 4]
                    if kind == "q":
                        self.S.wait(z)
                        z = self.S.ac(qT[:, n, :], cv_, ACT.Silu)
                        cfree[j % 2] = z
                        tk = transposed(qT[:, n, :], z, tb)
                        self.S.wait(tk)
                        for m in range(4):
                            z = self.S.ac(sqs, tb.ap[:, m * 128:(m + 1) * 128], ACT.Square, acc=ssq[:, m, n:n + 1])
                        tb.free = [z]
                    else:
                        self.S.wait(z)
                        z = self.S.ac(cv_, cv_, ACT.Silu)
                        tk = transposed(cv_, z, tb)
                        cfree[j % 2] = tk
                        tv = tb.ap.rearrange("p (t d) -> p t d", t=4)
                        if kind == "k":
                            self.S.wait(tk)
                            for m in range(4):
                                z = self.S.ac(sqs, tb.ap[:, m * 128:(m + 1) * 128], ACT.Square, acc=ssk[:, m, n:n + 1])
                            self.S.wait(tk)
                            z = self.S.cp(kt[:, :, n, :], tv)
                        else:
                            self.S.wait(tk)
                            z = self.S.cp(vt[:, :, n, :], tv)
                        tb.free = [z]
            for ss in (ssq, ssk):
                self.V.wait(z)
                z = self.V.ts(ss, ss, 1e-06, None, ALU.add, None)
                self.S.wait(z)
                z = self.S.ac(ss, ss, ACT.Sqrt)
                self.V.wait(z)
                z = self.V.rec(ss, ss)
            z = self.V.ts(ssq, ssq, float(128 ** (-0.5)), None, ALU.mult, None)
            for m in range(4):
                z = self.V.tt(kt[:, m], kt[:, m], ssk[:, m, :].unsqueeze(2).to_broadcast([128, 4, 128]), ALU.mult)
            self.P.wait(z)
            for n in range(4):
                tb = kb[n]
                self.P.wait(tb.free)
                for m in range(4):
                    self.P.tr(tb.ap[:, m * 128:(m + 1) * 128], kt[:, m, n, :])
                tk = self.P.done()
                q = self.either()
                q.wait(tk)
                f = q.cp(kT[:, n, :], tb.ap)
                tb.free = [f]
            self.stage()
            self.top = work
            seen = set()
            chains = [self.chain(half, hg, d, [self.banks[2 * (hg * 2 + d)], self.banks[2 * (hg * 2 + d) + 1]],
                                 qT, kT, kt, vt, O, lev, g, be, egc, erl, beg, egl, seen)
                      for hg in range(2) for d in range(2)]
            while chains:
                live = []
                for ch in chains:
                    if next(ch, None) is not None:
                        live.append(ch)
                chains = live
            self.stage()
            self.top = work
            zs = self.al(1024)
            oT = self.al2(8, 512)
            sq = self.al3(1, 8, 128)[:, 0]
            st = self.al2(4, 8)
            scr = self.al(512)
            for t in range(4):
                for n in range(8):
                    z = self.V.ts(O[:, t, n, :], O[:, t, n, :], ssq[:, t, n // 2:n // 2 + 1], None, ALU.mult, None)
                z = self.V.tt(sq, O[:, t], O[:, t], ALU.mult)
                z = self.V.red(st[:, t, :], sq, ALU.add)
            z = self.rstd(st, st, 128, z)
            for t in range(4):
                z = self.V.tt(O[:, t], O[:, t], st[:, t, :].unsqueeze(2).to_broadcast([128, 8, 128]), ALU.mult)
            self.zf = [None, None]

            def zgate(t, n0, nw, bank, tk):
                q = (n0 // 512 * 4 + t) % 2
                self.S.wait(tk, self.zf[q])
                zz = self.S.ac(zs[:, q * 512:q * 512 + 512], bank, ACT.Silu)
                ov = O[:, t].rearrange("p h d -> p (h d)")[:, n0:n0 + 512]
                self.V.wait(zz)
                self.zf[q] = self.V.tt(ov, ov, zs[:, q * 512:q * 512 + 512], ALU.mult)
                return zz

            self.proj_tok(hT, 8, W, 1024, 4, zgate, ht, base=4096 + half * 1024)
            self.P.wait(self.zf[0], self.zf[1])
            for t in range(4):
                for h0 in (0, 4):
                    tb = self.banks[(t * 2 + h0 // 4) % 8]
                    self.P.wait(tb.free)
                    for h in range(4):
                        self.P.tr(tb.ap[:, h * 128:(h + 1) * 128], O[:, t, h0 + h, :])
                    tk = self.P.done()
                    q = self.either()
                    dst = oT[:, h0:h0 + 4, t * 128:(t + 1) * 128]
                    srcv = tb.ap.rearrange("p (h n) -> p h n", h=4)
                    if q is self.S:
                        self.S.wait(tk)
                        f = self.S.ac(dst, srcv, ACT.Copy, scale=self.ng)
                    else:
                        self.V.wait(tk)
                        f = self.V.ts(dst, srcv, self.ng, None, ALU.mult, None)
                    tb.free = [f]
            ot = [self.S.last, self.V.last]
            gs = [self.gate_rows(0, 0, v, self.al(1024), self.V.last) for v in (1, 0)]
            Wo = self.i["dn_w_out"][0]
            bs = self.banks
            self.P.wait(ot)
            for k0 in range(0, 8, 2):
                s, w = self.wslot(Wo, half * 8 + k0, 2, 0, 1024)
                self.P.wait(s.tok)
                for t in range(4):
                    for nh in range(2):
                        bk = bs[t * 2 + nh]
                        self.P.wait(bk.free)
                        for k in range(2):
                            self.P.mm(bk.ap, oT[:, k0 + k, t * 128:(t + 1) * 128], w[:, k, nh * 512:(nh + 1) * 512],
                                      k0 + k == 0, k0 + k == 7)
                        tk = self.P.done()
                        bk.done = tk
                s.free = [tk]
            for t in range(4):
                for nh in range(2):
                    bk = bs[t * 2 + nh]
                    bk.free = [self.add_gated(0, 0, t, nh * 512, 512, bk.ap, bk.done, scr, gs)]

    def chain(self, half, hg, d, bk, qT, kT, kt, vt, O, lev, g, be, egc, erl, beg, egl, seen):
        bufs = [self.al3(1, 4, 128)[:, 0] for _ in range(8)]
        gL, D, DT, T, Pm, Xp, M1, S = bufs
        h0 = half * 8 + hg * 4
        le, gt, ge, lt = (self.const(n) for n in (("le", "gt", "ge", "lt") if d == 0 else ("ge", "lt", "le", "gt")))
        b0, b1 = bk
        v4 = lambda b: b.ap.rearrange("p (h n) -> p h n", h=4)
        pair = lambda a: a.rearrange("p (h n) -> p h n", h=2).unsqueeze(2).to_broadcast([128, 2, 2, 128])
        four = lambda a: a.rearrange("p (h r) n -> p h r n", h=2)
        rep = lambda a: a.unsqueeze(1).to_broadcast([128, 4, 128])
        V, Sc, G = self.V, self.S, self.G
        first = True
        sfree = None
        for n in ((0, 1, 2, 3) if d == 0 else (1, 0, 3, 2)):
            tok = slice(n * 128, (n + 1) * 128)
            col = lambda a: a[:, n, d, h0:h0 + 4].unsqueeze(2).to_broadcast([128, 4, 128])
            V.wait(b0.free)
            z1 = V.tt(gL, rep(gt), col(g), ALU.mult)
            yield 1
            self.P.wait(z1, b0.free)
            self.P.mm(b0.ap, le, gL.rearrange("p h n -> p (h n)"), True, True)
            t0 = self.P.done()
            self.P.wait(z1, b1.free)
            for h in range(4):
                self.P.mm(b1.ap[:, h * 128:(h + 1) * 128], gL[:, h, :], le, True, True)
            t1 = self.P.done()
            yield 1
            self.S.wait(t0)
            a0 = self.S.ac(D, v4(b0), ACT.Exp)
            self.S.wait(t1)
            a1 = self.S.ac(DT, v4(b1), ACT.Exp)
            G.wait(t1, sfree)
            z1 = G.tt(M1, rep(gt), col(be), ALU.mult)
            yield 1
            self.P.wait(a0)
            for q in range(2):
                kq = kT[:, hg * 2 + q, tok]
                self.P.mm(b0.ap[:, q * 128:(q + 1) * 128], kq, kq, True, True)
            t0 = self.P.done()
            self.P.wait(a1)
            for q in range(2):
                self.P.mm(b1.ap[:, q * 128:(q + 1) * 128], kT[:, hg * 2 + q, tok], qT[:, hg * 2 + q, tok], True, True)
            t1 = self.P.done()
            V.wait(a0, z1)
            z = V.tt(D, D, M1, ALU.mult)
            V.wait(a1)
            z2 = V.tt(DT, DT, rep(le), ALU.mult)
            yield 1
            V.wait(t0)
            z = V.tt(four(D), four(D), pair(b0.ap[:, 0:256]), ALU.mult)
            V.wait(t1)
            z2 = V.tt(four(DT), four(DT), pair(b1.ap[:, 0:256]), ALU.mult)
            b0.free, b1.free = [z], [z2]
            G.wait(z, z2)
            zc = G.tt(gL, D, rep(lev[:, d, :]), ALU.mult)
            yield 1
            self.P.wait(zc, b0.free)
            for h in range(4):
                self.P.tr(b0.ap[:, h * 128:(h + 1) * 128], gL[:, h, :])
            t0 = self.P.done()
            yield 1
            V.wait(zc)
            zt = V.tt(T, rep(self.ident), gL, ALU.subtract)
            V.wait(t0)
            zp = V.tt(Pm, rep(self.ident), v4(b0), ALU.subtract)
            b0.free = [zp]
            G.wait(t0, zt)
            zc = G.tt(gL, D, rep(lev[:, 2 + d, :]), ALU.mult)
            yield 1
            for l in range(1, 7):
                self.P.wait(zc, zp, b0.free)
                for h in range(4):
                    self.P.mm(b0.ap[:, h * 128:(h + 1) * 128], gL[:, h, :], Pm[:, h, :], True, True)
                t0 = self.P.done()
                yield 1
                Sc.wait(t0)
                zx = Sc.cp(Xp, v4(b0))
                b0.free = [zx]
                if l < 6:
                    G.wait(t0)
                    zc = G.tt(gL, D, rep(lev[:, 2 * l + 2 + d, :]), ALU.mult)
                yield 1
                self.P.wait(zx, zt, b1.free)
                for h in range(4):
                    self.P.mm(b1.ap[:, h * 128:(h + 1) * 128], T[:, h, :], Xp[:, h, :], True, True)
                t1 = self.P.done()
                yield 1
                V.wait(t1)
                zp = V.tt(Pm, Pm, v4(b1), ALU.subtract)
                b1.free = [zp]
                yield 1
                if l < 6:
                    self.P.wait(zp, b0.free)
                    for h in range(4):
                        self.P.tr(b0.ap[:, h * 128:(h + 1) * 128], Pm[:, h, :])
                    t0 = self.P.done()
                    yield 1
                    Sc.wait(t0)
                    zt = Sc.cp(T, v4(b0))
                    b0.free = [zt]
            kv = kt[:, n, hg * 2:hg * 2 + 2, :].unsqueeze(2).to_broadcast([128, 2, 2, 128])
            G.wait(zp)
            zk = G.tt(four(M1), kv,
                      beg[:, n, d, h0:h0 + 4].rearrange("p (a b) -> p a b",
                                                        a=2).unsqueeze(3).to_broadcast([128, 2, 2, 128]), ALU.mult)
            V.wait(zp)
            zv = V.tt(D, vt[:, n, hg * 4:hg * 4 + 4, :], col(be), ALU.mult)
            yield 1
            if not first:
                self.P.wait(zk, zp, b0.free)
                for h in range(4):
                    self.P.mm(b0.ap[:, h * 128:(h + 1) * 128], M1[:, h, :], Pm[:, h, :], True, True)
                t0 = self.P.done()
                self.S.wait(t0)
                zx = self.S.ac(Xp, v4(b0), ACT.Copy, scale=-1.0)
                b0.free = [zx]
                yield 1
            self.P.wait(zv, zp, b1.free)
            for h in range(4):
                o = b1.ap[:, h * 128:(h + 1) * 128]
                self.P.mm(o, Pm[:, h, :], D[:, h, :], True, first)
                if not first:
                    self.P.wait(zx, sfree)
                    self.P.mm(o, Xp[:, h, :], S[:, h, :], False, True)
            t1 = self.P.done()
            yield 1
            Sc.wait(t1)
            vn = Sc.cp(T, v4(b1))
            b1.free = [vn]
            G.wait(t1, t0)
            zk = G.tt(four(M1), kv,
                      erl[:, n, d, h0:h0 + 4].rearrange("p (a b) -> p a b",
                                                        a=2).unsqueeze(3).to_broadcast([128, 2, 2, 128]), ALU.mult)
            yield 1
            if not first:
                self.P.wait(sfree, b0.free)
                for h in range(4):
                    self.P.mm(b0.ap[:, h * 128:(h + 1) * 128], qT[:, hg * 2 + h // 2, tok], S[:, h, :], True, True)
                t0 = self.P.done()
            self.P.wait(vn, z2, b1.free)
            for h in range(4):
                self.P.mm(b1.ap[:, h * 128:(h + 1) * 128], DT[:, h, :], T[:, h, :], True, True)
            t1 = self.P.done()
            Ov = O[:, n, hg * 4:hg * 4 + 4, :]
            yield 1
            fresh = (hg, n) not in seen
            seen.add((hg, n))
            if not first:
                V.wait(t0, t1)
                z = V.tt(gL, v4(b0), col(egc), ALU.mult)
                b0.free = [z]
                if not fresh:
                    z = V.tt(Ov, Ov, gL, ALU.add)
                    V.wait(t1)
                    z = V.tt(Ov, Ov, v4(b1), ALU.add)
                else:
                    V.wait(t1)
                    z = V.tt(Ov, gL, v4(b1), ALU.add)
            elif fresh:
                V.wait(t1)
                z = V.cp(Ov, v4(b1))
            else:
                V.wait(t1)
                z = V.tt(Ov, Ov, v4(b1), ALU.add)
            b1.free = [z]
            yield 1
            self.P.wait(zk, vn, b0.free)
            for h in range(4):
                self.P.mm(b0.ap[:, h * 128:(h + 1) * 128], M1[:, h, :], T[:, h, :], True, True)
            t0 = self.P.done()
            yield 1
            if first:
                V.wait(t0)
                sfree = V.cp(S, v4(b0))
            else:
                V.wait(t0)
                z = V.tt(S, S, col(egl), ALU.mult)
                sfree = V.tt(S, S, v4(b0), ALU.add)
            b0.free = [sfree]
            first = False
            yield 1

    def peer(self, l, tiles):
        self.stage()
        GT = self.al2(128, 256)
        half8 = lambda a, n: a.bitcast(BF16).rearrange("p (k n) -> p k n", k=n)
        ub = self.al(2048)
        uh = [[half8(ub[:, (2 * n + w) * 512:(2 * n + w + 1) * 512], 8) for w in range(2)] for n in range(2)]
        vh = [[self.al(512).bitcast(BF16) for _ in range(2)] for _ in range(2)]
        hh = [half8(self.al(1024), 8) for _ in range(2)]
        ge = [self.al(256) for _ in range(2)]
        co = [[self.al(128).bitcast(BF16) for _ in range(2)] for _ in range(2)]
        iT, jT, gT = self.al(256), self.al(256), self.al(256)
        self.top = 0
        scr = self.al(3080)
        hT = self.al2(8, 256)
        A, B = self.mod_cols(l, 1, tiles)
        ht = self.norm_T(tiles, hT, A, B, scr)
        self.S.wait(ht)
        z = self.S.cp(hh[0], hT)
        self.V.wait(z)
        hp = self.V.tt(hh[1], hT, hh[0], ALU.subtract)
        skT = self.al2(16, 128)
        sc = self.al3(2, 16, 128)
        qs = [self.al(256) for _ in range(2)]
        qfree = [None, None]
        sk = self.load([(lambda a: a.rearrange("p (h d) -> p h d", h=16), self.i["peer_sub_keys"][l].rearrange("h c k d -> k (h c) d"))])
        skv = sk.ap.rearrange("p (h d) -> p h d", h=16)
        toks = []
        self.P.wait(sk.tok)
        for c0 in range(0, 16, 4):
            b = self.banks[4 + (c0 // 4) % 4]
            self.P.wait(b.free)
            for k in range(4):
                self.P.tr(b.ap[:, k * 128:(k + 1) * 128], skv[:, c0 + k, :])
            tk = self.P.done()
            q = self.either()
            q.wait(tk)
            f = q.cp(skT[:, c0:c0 + 4, :], b.ap.rearrange("p (k n) -> p k n", k=4))
            b.free = [f]
            toks.append(f)
        sk.free = [tk]
        st = toks[-2:]
        sbank = [self.banks[6], self.banks[7]]

        def score(c, bank, tk):
            self.S.wait(tk, qfree[c % 2])
            z = self.S.cp(qs[c % 2], bank[:, 0:256])
            b = self.banks[4 + c % 4]
            self.P.wait(z, st, b.free)
            for t in range(2):
                self.P.mm(b.ap[:, t * 128:(t + 1) * 128], qs[c % 2][:, t * 128:(t + 1) * 128], skT[:, c, :], True, True)
            tk = self.P.done()
            qfree[c % 2] = tk
            self.V.wait(tk)
            f = self.V.cp(sc[:, :, c, :], b.ap[:, 0:256].rearrange("p (t k) -> p t k", t=2))
            b.free = [f]
            return z

        self.proj_feat(hT, 8, self.i["peer_w_query"][l], 2048, 256, score, ht, banks=self.banks[0:4])
        mark = self.top
        outs = [self.al2(3, 128) for _ in range(2)]
        iota = self.const("iota")
        for t in range(2):
            self.top = mark + 768
            val, idx, idf = self.al2(16, 16), self.al2(16, 16).bitcast(U32), self.al2(16, 16)
            sw = self.al2(16, 128)
            for c in range(16):
                self.top16(sc[:, t, c, :], sw[:, c, :], val[:, c, :], idx[:, c, :])
            z = self.V.cp(idf, idx)
            cand = self.al3(8, 16, 16)
            vv = val.rearrange("p (h c) k -> p h c k", c=2)
            z = self.V.tt(cand, vv[:, :, 0, :].unsqueeze(3).to_broadcast([128, 8, 16, 16]),
                          vv[:, :, 1, :].unsqueeze(2).to_broadcast([128, 8, 16, 16]), ALU.add)
            best, pos = self.al2(8, 16), self.al2(8, 16).bitcast(U32)
            cw = self.al2(8, 256)
            for h in range(8):
                self.top16(cand[:, h].rearrange("p a b -> p (a b)"), cw[:, h, :], best[:, h, :], pos[:, h, :])
            nm, sm = self.al(8), self.al(8)
            self.V.cp(nm, best[:, :, 0])
            z = self.V.tt(best, best, nm.unsqueeze(2).to_broadcast([128, 8, 16]), ALU.subtract)
            self.S.wait(z)
            z = self.S.ac(best, best, ACT.Exp)
            self.V.wait(z)
            z = self.V.red(sm, best, ALU.add)
            z = self.V.rec(sm, sm)
            z = self.V.tt(outs[t][:, 2, :].rearrange("p (h k) -> p h k", h=8), best,
                          sm.unsqueeze(2).to_broadcast([128, 8, 16]), ALU.mult)
            pi = self.al(128).bitcast(U32)
            pf = self.al(128)
            eq = self.al3(8, 16, 16)
            iv = idf.rearrange("p (h c) k -> p h c k", c=2)
            pv = pos.rearrange("p h k -> p (h k)")
            for w in range(2):
                if w == 0:
                    z = self.V.ts(pi, pv, 4, None, ALU.logical_shift_right, None)
                else:
                    z = self.V.ts(pi, pv, 15, None, ALU.bitwise_and, None)
                z = self.V.cp(pf, pi)
                e3 = eq.rearrange("p h k a -> p (h k) a")
                z = self.V.tt(e3, pf.unsqueeze(2).to_broadcast([128, 128, 16]),
                              iota[:, 0:16].unsqueeze(1).to_broadcast([128, 128, 16]), ALU.is_equal)
                z = self.V.tt(eq, eq, iv[:, :, w, :].unsqueeze(2).to_broadcast([128, 8, 16, 16]), ALU.mult)
                z = self.V.red(outs[t][:, w, :], e3, ALU.add)
            b = self.banks[4 + t]
            self.P.wait(z, b.free)
            for w in range(3):
                self.P.tr(b.ap[:, w * 128:(w + 1) * 128], outs[t][:, w, :])
            tk = self.P.done()
            self.V.wait(tk)
            for w, dst in enumerate((iT, jT, gT)):
                z = self.V.cp(dst[:, t * 128:(t + 1) * 128], b.ap[:, w * 128:(w + 1) * 128])
            b.free = [z]
        fence = [z, self.P.done()]
        hot = [ub[:, n * 1024:(n + 1) * 1024].rearrange("p (a n) -> p a n", a=8) for n in range(2)]
        hfree = [None] * 8
        self.S.wait(fence)
        self.G.wait(fence[0])
        for p0 in range(0, 256, 4):
            b = self.banks[4 + (p0 // 4) % 4]
            self.P.wait(b.free)
            for p in range(p0, p0 + 4):
                q = p % 8
                hb = hot[q // 4]
                Bp, Ap = hb[:, 2 * (q % 4), :], hb[:, 2 * (q % 4) + 1, :]
                self.G.wait(hfree[q])
                zb = self.G.ts(Bp, iota, jT[:, p:p + 1], None, ALU.is_equal, None)
                self.V.wait(hfree[q])
                z = self.V.ts(Ap, iota, iT[:, p:p + 1], gT[:, p:p + 1], ALU.is_equal, ALU.mult)
                self.P.wait(z, zb)
                self.P.mm(b.ap[:, (p - p0) * 128:(p - p0 + 1) * 128], Bp, Ap, True, True)
                tk = self.P.done()
                hfree[q] = tk
            self.S.wait(tk)
            f = self.S.cp(GT[:, :, p0:p0 + 4], b.ap.rearrange("p (t i) -> p i t", t=4))
            b.free = [f]
        gt_t = [f, hfree[3], hfree[7]]
        yb, tb, ab = self.banks[0:4], self.banks[4:6], self.banks[6:8]
        ug, vg = self.i["peer_u"][l], self.i["peer_v"][l]
        slots, utok, vtok, ctok = {}, {}, {}, {}
        ufree, vfree, gfree, cfree = [gt_t, gt_t], [None, None], [None, None], [None, None]

        def fetch(i):
            s = self.load([(lambda a: a[:, 0:1024], ug[i * 128:(i + 1) * 128, :]),
                           (lambda a: a[:, 1024:2048], vg[i * 128:(i + 1) * 128, :])])
            uhi, ulo = uh[i % 2]
            fs = []
            self.S.wait(ufree[i % 2])
            self.P.wait(s.tok)
            for half in range(2):
                b = tb[half]
                self.P.wait(b.free)
                for k in range(4):
                    c = half * 4 + k
                    self.P.tr(b.ap[:, k * 128:(k + 1) * 128], s.ap[:, c * 128:(c + 1) * 128])
                tk = self.P.done()
                bv = b.ap.rearrange("p (k n) -> p k n", k=4)
                sl = slice(half * 4, half * 4 + 4)
                self.S.wait(tk)
                f = self.S.cp(uhi[:, sl, :], bv)
                self.V.wait(f)
                f = self.V.tt(ulo[:, sl, :], bv, uhi[:, sl, :], ALU.subtract)
                b.free = [f]
                fs.append(f)
            utok[i] = fs
            slots[i] = (s, tk)

        def split(i):
            s, tu = slots.pop(i)
            vhi, vlo = vh[i % 2]
            v = s.ap[:, 1024:2048]
            self.G.wait(s.tok, vfree[i % 2])
            f = self.G.cp(vhi, v)
            self.V.wait(f)
            vtok[i] = self.V.tt(vlo, v, vhi, ALU.subtract)
            s.free = [tu, vtok[i]]

        def act(i):
            b = ab[i % 2]
            uhi, ulo = uh[i % 2]
            self.P.wait(utok[i], hp, b.free)
            for k in range(8):
                for n, (x, y) in enumerate(((uhi, hh[0]), (uhi, hh[1]), (ulo, hh[0]))):
                    self.P.mm(b.ap[:, 0:256], x[:, k, :], y[:, k, :], k == 0 and n == 0, k == 7 and n == 2)
            tk = self.P.done()
            ufree[i % 2] = tk
            self.S.wait(tk, gfree[i % 2])
            z = self.S.ac(ge[i % 2], b.ap[:, 0:256], ACT.Gelu)
            b.free = [z]
            chi, clo = co[i % 2]
            self.V.wait(z)
            z = self.V.tt(ge[i % 2], ge[i % 2], GT[:, i, :], ALU.mult)
            self.S.wait(z, cfree[i % 2])
            z = self.S.cp(chi, ge[i % 2])
            self.V.wait(z)
            ctok[i] = self.V.tt(clo, ge[i % 2], chi, ALU.subtract)
            gfree[i % 2] = ctok[i]

        def mix(i):
            chi, clo = co[i % 2]
            vhi, vlo = vh[i % 2]
            self.P.wait(ctok[i], vtok[i])
            for t in range(2):
                ts_ = slice(t * 128, (t + 1) * 128)
                for n, (x, y) in enumerate(((chi, vhi), (chi, vlo), (clo, vhi))):
                    for nh in range(2):
                        bk = yb[t * 2 + nh]
                        self.P.wait(bk.free)
                        self.P.mm(bk.ap, x[:, ts_], y[:, nh * 512:(nh + 1) * 512], i == 0 and n == 0, i == 127 and n == 2)
            tk = self.P.done()
            cfree[i % 2] = vfree[i % 2] = tk
            return tk

        fetch(0)
        split(0)
        for i in range(128):
            if i + 1 < 128:
                fetch(i + 1)
            act(i)
            if i >= 1:
                mix(i - 1)
            if i + 1 < 128:
                split(i + 1)
        tk = mix(127)
        gs = [self.gate_rows(l, 1, 1 if tiles[0] < 2 else 0, ub[:, 1024:2048], tk)]
        s2 = ub[:, 0:512]
        for t in range(2):
            for nh in range(2):
                bk = yb[t * 2 + nh]
                bk.free = [self.add_gated(l, 1, tiles[t], nh * 512, 512, bk.ap, tk, s2, gs)]

    def top16(self, src, wrk, val, idx):
        V = self.V
        V.do(lambda e: e.max(val[:, 0:8], src))
        V.do(lambda e: e.max_index(idx[:, 0:8], val[:, 0:8], src))
        V.do(lambda e: e.match_replace(wrk, val[:, 0:8], src, -3.0e38))
        V.do(lambda e: e.max(val[:, 8:16], wrk))
        return V.do(lambda e: e.max_index(idx[:, 8:16], val[:, 8:16], wrk))

    def row_norm(self, x, heads, hd, gain, scr, st, ready=None):
        self.V.wait(ready)
        z = self.V.tt(scr, x, x, ALU.mult)
        z = self.V.red(st, scr, ALU.add)
        z = self.rstd(st, st, hd, z)
        z = self.V.tt(x, x, st.unsqueeze(2).to_broadcast([128, heads, hd]), ALU.mult)
        if gain is not None:
            z = self.V.tt(x, x, gain, ALU.mult)
        return z

    def softmax_av(self, sps, nk, P_, mx, sm, tk, pT, pt_bank, out_mm, scale=1.0):
        self.V.wait(tk)
        z = self.V.red(mx, sps, ALU.max)
        z = self.V.ts(mx, mx, -scale, None, ALU.mult, None)
        self.S.wait(z)
        z = self.S.ac(P_, sps, ACT.Exp, bias=mx, scale=scale, acc=sm)
        self.P.wait(z, pt_bank.free)
        for c in range(nk // 128):
            self.P.tr(pt_bank.ap[:, c * 128:(c + 1) * 128], P_[:, c * 128:(c + 1) * 128])
        t = self.P.done()
        self.S.wait(t)
        f = self.S.cp(pT[:, 0:nk], pt_bank.ap[:, 0:nk])
        pt_bank.free = [f]
        self.V.wait(z)
        r = self.V.rec(sm, sm)
        return f, r, z

    def attention(self):
        self.stage()
        W = self.i["att_w_in"][0]
        hT = self.al2(8, 512)
        scr = self.al(3080)
        A, B = self.mod_cols(1, 0, range(4))
        ht = self.norm_T(range(4), hT, A, B, scr)
        q, k, v = self.al2(2, 1024), self.al2(4, 256), self.al2(4, 256)
        gq, gk, cs = self.al(128), self.al(128), self.al(256)
        lane = Lane(self.sem("l_att"))
        self.G.dma(lane, gq, self.i["att_qn_g"][0].partition_broadcast(128))
        self.G.dma(lane, gk, self.i["att_kn_g"][0].partition_broadcast(128))
        o = self.off["cos"][0]
        lt = self.G.dma(lane, cs, self.i["consts"][:, o:o + 256])
        def qcols(t, n0, nw, b, tk):
            self.V.wait(tk)
            return self.V.cp(q[:, t, n0:n0 + nw], b)

        self.proj_tok(hT[:, :, 256:512], 8, W, 1024, 2, qcols, ht)

        def kv(t, n0, nw, b, tk):
            self.S.wait(tk)
            self.S.cp(k[:, t, :], b[:, 0:256])
            self.S.wait(tk)
            return self.S.cp(v[:, t, :], b[:, 256:512])

        self.proj_tok(hT, 8, W, 512, 4, kv, ht, base=1024)
        jt = [self.S.last, self.V.last]
        st = self.al(8)
        sq = self.al(1024)
        tmp = [self.al(512) for _ in range(4)]
        rot = self.al(1024)
        qT, kT = self.al2(8, 256), self.al2(2, 512)
        z = jt

        def rope(x, heads, t, out, z):
            xv = x.rearrange("p (h i e) -> p h i e", h=heads, e=2)
            ov = out[:, 0:heads * 128].rearrange("p (h i e) -> p h i e", h=heads, e=2)
            c = cs[:, t * 64:(t + 1) * 64].unsqueeze(1).to_broadcast([128, heads, 64])
            s = cs[:, 128 + t * 64:128 + (t + 1) * 64].unsqueeze(1).to_broadcast([128, heads, 64])
            m = [a[:, 0:heads * 64].rearrange("p (h i) -> p h i", h=heads) for a in tmp]
            self.V.wait(z)
            self.V.tt(m[0], xv[:, :, :, 0], c, ALU.mult)
            self.V.tt(m[1], xv[:, :, :, 1], s, ALU.mult)
            self.V.tt(m[2], xv[:, :, :, 0], s, ALU.mult)
            self.V.tt(m[3], xv[:, :, :, 1], c, ALU.mult)
            self.V.tt(ov[:, :, :, 0], m[0], m[1], ALU.subtract)
            return self.V.tt(ov[:, :, :, 1], m[2], m[3], ALU.add)

        rf = None
        for t in range(2):
            xq = q[:, t, :].rearrange("p (h d) -> p h d", h=8)
            z = self.row_norm(xq, 8, 128, gq.unsqueeze(1).to_broadcast([128, 8, 128]), sq.rearrange("p (h d) -> p h d", h=8), st, [z, lt])
            z = rope(q[:, t, :], 8, t, rot, rf)
            z = self.to_T(rot, 8, qT[:, :, t * 128:(t + 1) * 128], z)
            rf = self.P.done()
        for t in range(4):
            xk = k[:, t, :].rearrange("p (h d) -> p h d", h=2)
            z = self.row_norm(xk, 2, 128, gk.unsqueeze(1).to_broadcast([128, 2, 128]), sq[:, 0:256].rearrange("p (h d) -> p h d", h=2), st[:, 0:2], z)
            src = k[:, t, :]
            if t >= 2:
                z = rope(k[:, t, :], 2, t - 2, rot, rf)
                src = rot[:, 0:256]
            z = self.to_T(src, 2, kT[:, :, t * 128:(t + 1) * 128], z)
            rf = self.P.done()
        Ps, pTs = [self.al(512) for _ in range(2)], [self.al(512) for _ in range(2)]
        mx, sm = self.al(16), self.al(16)
        o = self.al2(2, 1024)
        of = [None, None]
        self.P.wait(z, jt)
        for n in range(16):
            t, h = n // 8, n % 8
            b = self.banks[n % 2]
            self.P.wait(b.free)
            self.P.mm(b.ap, qT[:, h, t * 128:(t + 1) * 128], kT[:, h // 4, :], True, True)
            tk = self.P.done()
            f, r, e = self.softmax_av(b.ap, 512, Ps[n % 2], mx[:, n:n + 1], sm[:, n:n + 1], tk, pTs[n % 2], self.banks[2 + n % 2], None, scale=float(128 ** -0.5))
            b.free = [e]
            ob = self.banks[4 + n % 4]
            self.P.wait(f, ob.free)
            for c in range(4):
                self.P.mm(ob.ap[:, 0:128], pTs[n % 2][:, c * 128:(c + 1) * 128], v[:, c, h // 4 * 128:(h // 4 + 1) * 128],
                          c == 0, c == 3)
            tk = self.P.done()
            self.S.wait(tk)
            self.V.wait(tk, r)
            f = self.V.ts(o[:, t, h * 128:(h + 1) * 128], ob.ap[:, 0:128], sm[:, n:n + 1], None, ALU.mult, None)
            ob.free = [f]
        oT = self.al2(8, 256)
        for t in range(2):
            z = self.to_T(o[:, t, :], 8, oT[:, :, t * 128:(t + 1) * 128], f)
        gs = [self.gate_rows(1, 0, 0, self.al(1024))]

        def out_cols(t, n0, nw, b, tk):
            return self.add_gated(1, 0, t + 2, n0, nw, b, tk, sq, gs)

        self.proj_tok(oT, 8, self.i["att_w_out"][0], 1024, 2, out_cols, z)

    def final_norm(self):
        self.stage()
        g = self.al(1024)
        sq = self.al(1024)
        st = self.al(2)
        lt = self.misc(g, self.i["final_g"].partition_broadcast(128))
        self.V.wait(lt)
        for t in range(2):
            x = self.X[:, t + 2, :]
            z = self.S.ac(sq, x, ACT.Square, acc=st[:, t:t + 1])
            z = self.rstd(st[:, t:t + 1], st[:, t:t + 1], 1024, z)
            self.V.wait(z)
            z = self.V.stt(x, x, st[:, t:t + 1], g, ALU.mult, ALU.mult)
        self.S.wait(z)
        self.P.wait(z)

    def gain_cols(self, name, l):
        a = self.vec(name, l)
        return [a, a]

    def even_mixer(self):
        self.stage()
        W = self.i["ev_w_in_2"][0]
        hT = self.al2(8, 256)
        scr = self.al(3080)
        ht = self.norm_T([2, 3], hT, self.gain_cols("norm_mix_2", 0), None, scr)
        u, va, q, k, vb = (self.al2(2, 512) for _ in range(5))
        f8 = self.al2(2, 8)
        vg, qg, kg, fb, ws = self.al(512), self.al(64), self.al(64), self.al(8), self.al2(4, 128)
        causal = self.al2(2, 256)
        lane = Lane(self.sem("l_ev"))
        for dst, src in ((vg, "ev_v_norm_2"), (qg, "ev_q_norm_2"), (kg, "ev_k_norm_2"), (fb, "ev_b_fgate_2")):
            self.G.dma(lane, dst, self.i[src][0].partition_broadcast(128))
        self.G.dma(lane, ws, self.i["ev_w_spatial_2"][0].rearrange("g t s -> t g s"))
        co = self.off["causal"][0]
        lt = self.G.dma(lane, causal, self.i["consts"][:, co:co + 512].rearrange("p (a b) -> p a b", a=2))
        dst = [u, va, q, k, vb]

        def cb(t, n0, nw, b, tk):
            n = n0 // 512
            if n < 2:
                self.S.wait(tk)
                return self.S.ac(dst[n][:, t, :], b, ACT.Gelu_apprx_tanh)
            if n < 5:
                self.V.wait(tk)
                return self.V.cp(dst[n][:, t, :], b)
            self.V.wait(tk)
            return self.V.cp(f8[:, t, :], b[:, 0:8])

        self.proj_tok(hT, 8, W, 2568, 2, cb, ht)
        jt = [self.S.last, self.V.last]
        sq, st = self.al(512), self.al(8)
        y = self.al2(2, 1024)
        wT = self.al2(4, 128)
        b = self.banks[0]
        self.P.wait(lt, b.free)
        for g in range(4):
            self.P.tr(b.ap[:, g * 128:(g + 1) * 128], ws[:, g, :])
        tk = self.P.done()
        self.V.wait(tk)
        z = self.V.tt(wT, b.ap.rearrange("p (g t) -> p g t", g=4), self.const("le").unsqueeze(1).to_broadcast([128, 4, 128]),
                      ALU.mult)
        b.free = [z]
        v4 = sq.rearrange("p (h d) -> p h d", h=4)
        for t in range(2):
            z = self.row_norm(va[:, t, :].rearrange("p (h d) -> p h d", h=4), 4, 128, vg.rearrange("p (h d) -> p h d", h=4), v4, st[:, 0:4], [jt, lt])
        self.P.wait(z)
        for t in range(2):
            b = self.banks[1 + t]
            self.P.wait(b.free)
            for g in range(4):
                self.P.mm(b.ap[:, g * 128:(g + 1) * 128], wT[:, g, :], va[:, t, g * 128:(g + 1) * 128], True, True)
            tk = self.P.done()
            self.V.wait(tk)
            for g in range(4):
                sl = slice(g * 128, (g + 1) * 128)
                f = self.V.stt(y[:, t, sl], b.ap[:, sl], self.vc[:, 89 + g:90 + g], u[:, t, sl], ALU.add, ALU.mult)
            b.free = [f]
        sp, lf, c8 = self.al2(2, 8), self.al2(2, 8), self.al2(2, 8)
        self.V.wait(jt)
        z = self.V.tt(lf, f8, fb.unsqueeze(1).to_broadcast([128, 2, 8]), ALU.add)
        z = self.V.ts(lf, lf, -1.0, None, ALU.mult, None)
        self.S.wait(z)
        z = self.S.ac(sp, lf, ACT.Abs)
        z = self.S.ac(sp, sp, ACT.Exp, scale=-1.0)
        self.V.wait(z)
        z = self.V.ts(sp, sp, 1.0, None, ALU.add, None)
        self.S.wait(z)
        z = self.S.ac(sp, sp, ACT.Ln)
        self.V.wait(z)
        z = self.V.stt(lf, lf, 0.0, sp, ALU.max, ALU.add)
        z = self.V.ts(lf, lf, -1.0, None, ALU.mult, None)
        b = self.banks[3]
        self.P.wait(z, b.free)
        self.P.mm(b.ap[:, 0:8], self.const("le"), lf[:, 0, :], True, True)
        self.P.mm(b.ap[:, 8:16], self.const("ones"), lf[:, 0, :], True, False)
        self.P.mm(b.ap[:, 8:16], self.const("le"), lf[:, 1, :], False, True)
        tk = self.P.done()
        self.V.wait(tk)
        z = self.V.cp(c8, b.ap[:, 0:16].rearrange("p (t h) -> p t h", t=2))
        self.P.wait(z)
        for t in range(2):
            self.P.tr(b.ap[0:8, 128 + t * 128:256 + t * 128], c8[:, t, :])
        tk = self.P.done()
        cT = self.al(256)
        self.V.wait(tk)
        z = self.V.ts(cT[0:8, :], b.ap[0:8, 128:384], -1.0, None, ALU.mult, None)
        b.free = [z]
        ctk = z
        sel = self.al2(8, 128)
        so = self.off["sel"][0]
        slt = self.misc(sel[0:8], self.i["consts"][0:8, so:so + 1024].rearrange("p (a b) -> p a b", a=8))
        qT, kT = self.al2(4, 256), self.al2(4, 256)
        s8 = sq.rearrange("p (h d) -> p h d", h=8)
        for x, gn, xT in ((q, qg, qT), (k, kg, kT)):
            for t in range(2):
                z = self.row_norm(x[:, t, :].rearrange("p (h d) -> p h d", h=8), 8, 64, gn.unsqueeze(1).to_broadcast([128, 8, 64]), s8, st)
                if x is q:
                    z = self.V.ts(x[:, t, :], x[:, t, :], 0.125, None, ALU.mult, None)
                z = self.to_T(x[:, t, :], 4, xT[:, :, t * 128:(t + 1) * 128], z)
        Ss, Ps, pTs = ([self.al(256) for _ in range(2)] for _ in range(3))
        mx, sm = self.al(16), self.al(16)
        self.P.wait(z, ctk, slt, jt)
        self.V.wait(lt, self.S.last)
        for n in range(16):
            t, h = n // 8, n % 8
            nk = 128 * (t + 1)
            b = self.banks[n % 2]
            r0 = 64 * (h % 2)
            self.P.wait(b.free)
            self.P.mm(b.ap[:, 0:nk], qT[r0:r0 + 64, h // 2, t * 128:(t + 1) * 128], kT[r0:r0 + 64, h // 2, 0:nk], True,
                      False)
            self.P.mm(b.ap[:, 0:nk], sel[0:8, h, :], cT[0:8, 0:nk], False, True)
            tk = self.P.done()
            self.V.wait(tk)
            f = self.V.stt(Ss[n % 2][:, 0:nk], b.ap[:, 0:nk], c8[:, t, h:h + 1], causal[:, t, 0:nk], ALU.add, ALU.add)
            b.free = [f]
            f, r, e = self.softmax_av(Ss[n % 2][:, 0:nk], nk, Ps[n % 2][:, 0:nk], mx[:, n:n + 1], sm[:, n:n + 1], f, pTs[n % 2], self.banks[2 + n % 2], None)
            ob = self.banks[4 + n % 4]
            self.P.wait(f, ob.free)
            for c in range(t + 1):
                self.P.mm(ob.ap[:, 0:64], pTs[n % 2][:, c * 128:(c + 1) * 128], vb[:, c, h * 64:(h + 1) * 64], c == 0,
                          c == t)
            tk = self.P.done()
            self.S.wait(tk)
            self.V.wait(tk, r)
            f = self.V.ts(y[:, t, 512 + h * 64:512 + (h + 1) * 64], ob.ap[:, 0:64], sm[:, n:n + 1], None, ALU.mult, None)
            ob.free = [f]
        yT = self.al2(8, 256)
        for t in range(2):
            z = self.to_T(y[:, t, :], 8, yT[:, :, t * 128:(t + 1) * 128], f)
        self.proj_tok(yT, 8, self.i["ev_w_out_2"][0], 1024, 2, self.add_x, z)

    def add_x(self, t, n0, nw, b, tk):
        x = self.X[:, t + 2, n0:n0 + nw]
        self.V.wait(tk)
        return self.V.tt(x, x, b[:, 0:nw], ALU.add)

    def ffn(self, l):
        self.stage()
        hT = self.al2(8, 256)
        scr = self.al(3080)
        ht = self.norm_T([2, 3], hT, self.gain_cols("norm_ffn_2", l), None, scr)
        cr = self.al(5632)
        cw = self.al2(44, 4)
        lane = Lane(self.sem(f"l_ffn{l}"))
        self.G.dma(lane, cr[0:3, :], self.i["ffn_conv_w_2"][l])
        t = self.G.dma(lane, cr[3:4, :], self.i["ffn_conv_b_2"][l].unsqueeze(0))
        b = self.banks[7]
        self.P.wait(t, b.free)
        for c in range(44):
            self.P.tr(b.ap[:, c * 4:c * 4 + 4], cr[0:4, c * 128:(c + 1) * 128])
        tk = self.P.done()
        self.V.wait(tk)
        z = self.V.cp(cw, b.ap[:, 0:176].rearrange("p (a b) -> p a b", a=44))
        b.free = [z]
        aT = self.al2(22, 256)
        accs = [self.al(256) for _ in range(3)]
        af = [None] * 3

        def cb(c, bank, tk):
            a = accs[c % 3]
            self.V.wait(tk, af[c % 3])
            z = self.V.ts(a, bank[:, 0:256], cw[:, c, 2:3], cw[:, c, 3:4], ALU.mult, ALU.add)
            z = self.V.stt(a[:, 1:256], bank[:, 0:255], cw[:, c, 1:2], a[:, 1:256], ALU.mult, ALU.add)
            z = self.V.stt(a[:, 2:256], bank[:, 0:254], cw[:, c, 0:1], a[:, 2:256], ALU.mult, ALU.add)
            if c < 22:
                self.S.wait(z)
                af[c % 3] = self.S.ac(aT[:, c, :], a, ACT.Silu)
            else:
                self.V.wait(self.S.last)
                af[c % 3] = self.V.tt(aT[:, c - 22, :], aT[:, c - 22, :], a, ALU.mult)
            return z

        self.proj_feat(hT, 8, self.i["ffn_w_up_2"][l], 5632, 256, cb, ht, banks=self.banks[0:4])
        at = self.V.last
        self.proj_tok(aT, 22, self.i["ffn_w_down_2"][l], 1024, 2, self.add_x, at, banks=self.banks[4:8])

    def ple(self, l):
        self.stage()
        hT = self.al2(8, 256)
        scr = self.al(3080)
        one = self.const("ones")[:, 0:8]
        ht = self.norm_T([2, 3], hT, [one, one], None, scr)
        p = self.al2(2, 256)
        pT = self.al2(2, 256)
        lt = self.misc(p, self.i["p_2"][l, 0].rearrange("(t p) d -> p t d", p=128))
        for t in range(2):
            z = self.to_T(p[:, t, :], 2, pT[:, :, t * 128:(t + 1) * 128], lt)
        pr = self.al2(2, 1024)

        def pcols(t, n0, nw, b, tk):
            self.V.wait(tk)
            return self.V.cp(pr[:, t, n0:n0 + nw], b)

        self.proj_tok(pT, 2, self.i["ple_w_proj_2"][l], 1024, 2, pcols, z)
        gt = [self.al(512) for _ in range(2)]
        gf = [None, None]

        def cb(t, n0, nw, b, tk):
            self.S.wait(tk, gf[t])
            z = self.S.ac(gt[t], b, ACT.Sigmoid)
            self.V.wait(z)
            self.V.tt(gt[t], gt[t], pr[:, t, n0:n0 + nw], ALU.mult)
            x = self.X[:, t + 2, n0:n0 + nw]
            gf[t] = self.V.tt(x, x, gt[t], ALU.add)
            return z

        self.proj_tok(hT, 8, self.i["ple_w_gate_2"][l], 1024, 2, cb, ht)

    def s5(self):
        self.stage()
        V, S, G = self.V, self.S, self.G
        M, AD, SU = ALU.mult, ALU.add, ALU.subtract
        hT = self.al2(8, 256)
        scr = self.al(3080)
        ht = self.norm_T([2, 3], hT, self.gain_cols("norm_mix_2", 1), None, scr)
        par = self.al2(3, 32)
        mag, th, k, sn, cs, t1, t2, den, cr, ci, nr, ni = (self.al(32) for _ in range(12))
        Er, Ei = self.al2(32, 256), self.al2(32, 256)
        BT = [self.al2(8, 128) for _ in range(2)]
        CT = [self.al2(8, 128) for _ in range(2)]
        low = self.top
        rows = self.al2(3, 128)
        ld = self.al(2)
        lane = Lane(self.sem("l_s5"))
        G.dma(lane, rows[0:32, 0, :], self.i["od_a_re_2"][0].rearrange("(j g) p -> j (g p)", g=2))
        G.dma(lane, rows[0:32, 1, :], self.i["od_a_im_2"][0].rearrange("(j g) p -> j (g p)", g=2))
        lt = G.dma(lane, ld[0:32, :], self.i["od_log_dt_2"][0].rearrange("(j g) -> j g", g=2))
        V.wait(lt)
        z = V.cp(rows[0:32, 2, :].rearrange("p (g s) -> p g s", g=2), ld[0:32, :].unsqueeze(2).to_broadcast([32, 2, 64]))
        b = self.banks[0]
        self.P.wait(z, b.free)
        for n in range(3):
            self.P.tr(b.ap[:, n * 32:(n + 1) * 32], rows[0:32, n, :])
        tk = self.P.done()
        V.wait(tk)
        z = V.cp(par, b.ap[:, 0:96].rearrange("p (a b) -> p a b", a=3))
        b.free = [z]
        lr, li, dt = par[:, 0, :], par[:, 1, :], par[:, 2, :]
        self.S.wait(z)
        z = self.S.ac(dt, dt, ACT.Exp)
        V.wait(z)
        z = V.tt(mag, lr, dt, M)
        self.S.wait(z)
        z = self.S.ac(mag, mag, ACT.Exp)
        z = V.tt(th, li, dt, M)
        z = V.ts(k, th, float(1 / (2 * np.pi)), 12582912.0, M, AD)
        z = V.ts(k, k, 12582912.0, None, SU, None)
        c1 = 6.28125
        z = self.V.stt(th, k, -c1, th, M, AD)
        z = self.V.stt(th, k, float(-(2 * np.pi - c1)), th, M, AD)
        lim = 3.1415925
        z = V.ts(th, th, lim, -lim, ALU.min, ALU.max)
        self.S.wait(z)
        za = self.S.ac(sn, th, ACT.Sin)
        self.S.wait(z)
        z = self.S.ac(cs, th, ACT.Abs)
        V.wait(z)
        z = V.ts(cs, cs, -1.0, float(np.pi / 2), M, AD)
        self.S.wait(z)
        z = self.S.ac(cs, cs, ACT.Sin)
        V.wait(z)
        z = V.tt(nr, mag, cs, M)
        z = V.ts(nr, nr, -1.0, None, AD, None)
        z = V.tt(ni, mag, sn, M)
        z = V.tt(den, lr, lr, M)
        z = V.tt(t1, li, li, M)
        z = V.tt(den, den, t1, AD)
        z = self.V.rec(den, den)
        for dst, a, c, op in ((cr, nr, ni, AD), (ci, ni, nr, SU)):
            z = V.tt(t1, a, lr, M)
            z = V.tt(t2, c, li, M)
            z = V.tt(dst, t1, t2, op)
            z = V.tt(dst, dst, den, M)
        bre, bim = self.al2(32, 16), self.al2(32, 16)
        lane = Lane(self.sem("l_s5b"))
        G.dma(lane, bre, self.i["od_b_re_2"][0].rearrange("(j g) p c -> (g p) j c", g=2))
        lt = G.dma(lane, bim, self.i["od_b_im_2"][0].rearrange("(j g) p c -> (g p) j c", g=2))
        bb = [self.al3(32, 2, 16) for _ in range(2)]
        t16 = [self.al2(32, 16) for _ in range(2)]
        crb, cib = cr.unsqueeze(2).to_broadcast([128, 32, 16]), ci.unsqueeze(2).to_broadcast([128, 32, 16])
        pm = self.const("par")
        V.wait(lt)
        for n, (a, c, op) in enumerate(((bre, bim, SU), (bim, bre, AD))):
            z = V.tt(t16[0], a, crb, M)
            z = V.tt(t16[1], c, cib, M)
            z = V.tt(t16[0], t16[0], t16[1], op)
            for g2 in range(2):
                z = V.ts(bb[n][:, :, g2, :], t16[0], pm[:, 2 + g2:3 + g2], None, M, None)
        for n in range(2):
            z2 = self.to_T(bb[n].rearrange("p j g c -> p (j g c)"), 8, BT[n], z)
        cc = [self.al2(8, 64) for _ in range(2)]
        cz = [self.al3(8, 2, 64) for _ in range(2)]
        lane = Lane(self.sem("l_s5c"))
        G.dma(lane, cc[0], self.i["od_c_re_2"][0].rearrange("(q g) c p -> (g c) q p", g=8))
        lt = G.dma(lane, cc[1], self.i["od_c_im_2"][0].rearrange("(q g) c p -> (g c) q p", g=8))
        V.wait(lt)
        for n in range(2):
            for g2 in range(2):
                z = V.ts(cz[n][:, :, g2, :], cc[n], pm[:, g2:g2 + 1], (1.0, -1.0)[n], M, M)
            z2 = self.to_T(cz[n].rearrange("p q g s -> p (q g s)"), 8, CT[n], z)
        z = V.ms(Er[:, :, 0:1], 1.0)
        z = V.ms(Ei[:, :, 0:1], 0.0)
        z = V.cp(Er[:, :, 1], cs)
        z = V.cp(Ei[:, :, 1], sn)
        self.top = low
        tm = [self.al(32 * 128) for _ in range(2)]
        V.wait(z2)
        for q in range(1, 8):
            w = 1 << q
            half = w // 2
            hr, hi = Er[:, :, half], Ei[:, :, half]
            z = V.tt(t1, hr, hr, M)
            z = V.tt(t2, hi, hi, M)
            z = V.tt(Er[:, :, w], t1, t2, SU)
            z = V.tt(t1, hr, hi, M)
            z = V.ts(Ei[:, :, w], t1, 2.0, None, M, None)
            wr = Er[:, :, w:w + 1].to_broadcast([128, 32, w - 1])
            wi = Ei[:, :, w:w + 1].to_broadcast([128, 32, w - 1])
            m = [a[:, 0:32 * (w - 1)].rearrange("p (j t) -> p j t", j=32) for a in tm]
            for dst, x, y_, op in ((Er, Er, Ei, SU), (Ei, Ei, Er, AD)):
                z = V.tt(m[0], x[:, :, 1:w], wr, M)
                z = V.tt(m[1], y_[:, :, 1:w], wi, M)
                z = V.tt(dst[:, :, w + 1:2 * w], m[0], m[1], op)
        gy = scr[:, 0:2048].rearrange("p (k t) -> p k t", k=8)
        a1 = [tm[0][:, n * 1024:n * 1024 + 512].rearrange("p (c t) -> p c t", c=2) for n in range(4)]
        a2 = [tm[0][:, n * 1024 + 512:n * 1024 + 1024].rearrange("p (c t) -> p c t", c=2) for n in range(4)]
        w2 = [tm[1][:, n * 1024:n * 1024 + 512].rearrange("p (c t) -> p c t", c=2) for n in range(4)]
        x2 = [tm[1][:, n * 1024 + 512:n * 1024 + 1024].rearrange("p (c t) -> p c t", c=2) for n in range(4)]
        xfree, pool, done = [None] * 4, [None] * 4, {}
        two = lambda a: a.unsqueeze(1).to_broadcast([128, 2, 256])

        def drive(j):
            q, jj = j // 4, j % 4
            rs = slice(32 * jj, 32 * jj + 32)
            b = self.banks[j % 4]
            self.P.wait(z2, ht, b.free)
            for n in range(2):
                self.P.mm(b.ap[:, n * 256:(n + 1) * 256], BT[n][rs, q, :], hT[rs, q, :], True, True, at=(32 * jj, 0))
            tk = self.P.done()
            b.done = tk

        drive(0)
        drive(1)
        self.P.wait(z2)
        for j in range(32):
            q, jj = j // 4, j % 4
            yb = self.banks[4 + q % 2]
            rs = slice(32 * jj, 32 * jj + 32)
            b = self.banks[j % 4]
            if j + 2 < 32:
                drive(j + 2)
            bv = b.ap.rearrange("p (c t) -> p c t", c=2)
            er, ei = Er[:, j, :], Ei[:, j, :]
            A_, B_, w_, x_ = a1[jj], a2[jj], w2[jj], x2[jj]
            V.wait(b.done, pool[jj])
            V.tt(A_, bv, two(er), M)
            z = V.tt(B_, bv, two(ei), M)
            b.free = [z]
            V.tt(A_[:, 0, :], A_[:, 0, :], B_[:, 1, :], AD)
            V.tt(A_[:, 1, :], A_[:, 1, :], B_[:, 0, :], SU)
            mg = mag[:, j:j + 1].to_broadcast([128, 256])
            for n in range(2):
                z = V.scan(w_[:, n, :], mg, A_[:, n, :])
            G.wait(z)
            G.tt(A_, w_, two(er), M)
            G.tt(B_, w_, two(ei), M)
            G.wait(xfree[jj])
            G.tt(x_[:, 0, :], A_[:, 0, :], B_[:, 1, :], SU)
            z = G.tt(x_[:, 1, :], A_[:, 1, :], B_[:, 0, :], AD)
            pool[jj] = z
            self.P.wait(z, yb.free)
            for n in range(2):
                self.P.mm(yb.ap[rs, 0:256], CT[n][:, q, rs], x_[:, n, :], n == 0, n == 1, at=(0, 32 * jj))
            tk = self.P.done()
            xfree[jj] = tk
            if jj == 3:
                done[q] = tk
            for c in ([q - 1] if jj == 1 and q else []) + ([7] if j == 31 else []):
                yc = self.banks[4 + c % 2]
                self.V.wait(done[c])
                z = self.V.stt(gy[:, c, :], hT[:, c, :], self.vec("od_d_2", 0)[:, c:c + 1], yc.ap[:, 0:256], M, AD)
                yc.free = [z]
        self.S.wait(z)
        z = self.S.ac(gy, gy, ACT.Gelu_apprx_tanh)
        ga = Er.rearrange("p j t -> p (j t)")[:, 0:2048].rearrange("p (t d) -> p t d", t=2)
        sg = [Ei.rearrange("p j t -> p (j t)")[:, n * 512:(n + 1) * 512] for n in range(2)]
        gf = [None, None]

        def cb(t, n0, nw, b, tk):
            if n0 < 1024:
                self.V.wait(tk)
                return self.V.cp(ga[:, t, n0:n0 + nw], b)
            n1 = n0 - 1024
            self.S.wait(tk, gf[t])
            z = self.S.ac(sg[t], b, ACT.Sigmoid)
            self.V.wait(z)
            self.V.tt(sg[t], sg[t], ga[:, t, n1:n1 + nw], ALU.mult)
            x = self.X[:, t + 2, n1:n1 + nw]
            gf[t] = self.V.tt(x, x, sg[t], ALU.add)
            return z

        self.S.wait(self.V.last)
        self.proj_tok(gy, 8, self.i["od_w_glu_2"][0], 2048, 2, cb, z)

    def end(self):
        self.stage()
        lane = Lane(self.sem("l_out"))
        self.SP.wait(self.V.last)
        t = self.SP.dma(lane, self.out[0].rearrange("(t p) d -> p t d", p=128), self.X[:, 2:4, :])
        self.SP.wait(t)

    def run(self):
        block = self.ctx.enter_context(self.nc.Block())

        @block.tensor
        def _(e):
            self.P.emit(e)

        @block.vector
        def _(e):
            self.V.emit(e)

        @block.scalar
        def _(e):
            self.S.emit(e)

        @block.gpsimd
        def _(e):
            self.G.emit(e)

        @block.sync
        def _(e):
            self.SP.emit(e)


def build(nc, ins, out, stages=None):
    with ExitStack() as ctx:
        p = Model(nc, ins, out, ctx)
        p.begin()
        p.ng = p.vc[:, 88:89]
        for name, args in (("ada", ()), ("deltanet", ()), ("peer", (0, (0, 1))), ("peer", (0, (2, 3))), ("attention", ()),
                           ("peer", (1, (2, 3))), ("final_norm", ()), ("even_mixer", ()), ("ffn", (0,)), ("ple", (0,)),
                           ("s5", ()), ("ffn", (1,)), ("ple", (1,))):
            if stages is None or name in stages:
                {"ada": p.ada, "deltanet": p.deltanet, "peer": p.peer, "attention": p.attention,
                 "final_norm": p.final_norm, "even_mixer": p.even_mixer, "ffn": p.ffn, "ple": p.ple, "s5": p.s5}[name](*args)
        p.end()
        p.run()


_INS = ["x", "c", "ctx", "c_ctx", "ada_w", "ada_b", "norm1_g", "norm2_g", "final_g", "dn_w_in", "dn_conv_w", "dn_a_log",
        "dn_dt_bias", "dn_norm_g", "dn_w_out", "att_w_in", "att_qn_g", "att_kn_g", "att_w_out", "peer_w_query",
        "peer_sub_keys", "peer_u", "peer_v", "p_2", "norm_mix_2", "norm_ffn_2", "ev_w_in_2", "ev_b_fgate_2",
        "ev_q_norm_2", "ev_k_norm_2", "ev_v_norm_2", "ev_w_spatial_2", "ev_b_spatial_2", "ev_w_out_2", "od_a_re_2",
        "od_a_im_2", "od_log_dt_2", "od_b_re_2", "od_b_im_2", "od_c_re_2", "od_c_im_2", "od_d_2", "od_w_glu_2",
        "ffn_w_up_2", "ffn_conv_w_2", "ffn_conv_b_2", "ffn_w_down_2", "ple_w_proj_2", "ple_w_gate_2"]


def kernel(**inputs):
    import concourse.bacc as _bacc
    from concourse.bass_utils import run_bass_kernel_spmd as _run

    nc = _bacc.Bacc("TRN2", target_bir_lowering=False, num_devices=1)
    arrays, args = {}, {}
    given = {name: np.ascontiguousarray(inputs[name]) for name in _INS}
    given["consts"] = constants()[0]
    for name, a in given.items():
        arrays[f"in_{name}"] = a
        args[name] = nc.dram_tensor(f"in_{name}", a.shape, mybir.dt.from_np(a.dtype), kind="ExternalInput").ap()
    out = nc.dram_tensor("out_0", (1, 256, 1024), F32, kind="ExternalOutput").ap()
    build(nc, args, out)
    r = _run(nc, [arrays], core_ids=[0])
    return r.results[0]["out_0"]
```

```python
from contextlib import ExitStack

import numpy as np

import concourse.bass as bass
import concourse.mybir as mybir

F32 = mybir.dt.float32
BF16 = mybir.dt.bfloat16
U32 = mybir.dt.uint32
ALU = mybir.AluOpType
ACT = mybir.ActivationFunctionType
AX = mybir.AxisListType.X

SPAN = 4000


class Engine:

    def __init__(self, name, new_sem):
        self.name, self.new_sem = name, new_sem
        self.items, self.nsem, self.made = [], 0, {}
        self.last = None

    def wait(self, *marks):
        for m in marks:
            if isinstance(m, list):
                self.wait(*m)
            elif m is not None and self.made.get(m[0], 0) < m[1]:
                self.made[m[0]] = m[1]
                self.items.append(("wait", m[0], m[1]))

    def count(self, at=-1):
        if self.last is None or self.last[1] == SPAN:
            self.last = (self.new_sem(f"s_{self.name}{self.nsem}"), 0)
            self.nsem += 1
        self.last = (self.last[0], self.last[1] + 1)
        self.items[at] = ("inc", self.items[at][1], self.last[0], 1)
        return self.last

    def dma(self, lane, out, in_):
        lane.n += 16
        self.items.append(("inc", lambda e: e.dma_start(out, in_), lane.sem, 16))
        return lane.sem, lane.n

    def emit(self, eng):
        for item in self.items:
            if item[0] == "wait":
                eng.wait_ge(item[1], item[2])
            elif item[0] == "inc":
                item[1](eng).then_inc(item[2], item[3])
            else:
                item[1](eng)


class Tensor(Engine):

    def do(self, fn):
        self.at, self.counted = len(self.items), False
        self.items.append(("do", fn))

    def done(self):
        if not self.counted:
            self.counted = True
            self.count(self.at)
        return self.last

    def mm(self, out, l, r, start, stop, at=None):
        if at is None:
            self.do(lambda e: e.matmul(out, l, r, start=start, stop=stop))
        else:
            self.do(lambda e: e.matmul(out, l, r, start=start, stop=stop, tile_position=at))

    def tr(self, out, in_):
        n = in_.shape[0]
        self.do(lambda e: e.transpose(out, in_, self.ident[0:n, 0:n]))


class Lanes(Engine):

    def do(self, fn, apart=False):
        if self.last is not None and not apart:
            self.wait(self.last)
        self.items.append(("do", fn))
        return self.count()

    def cp(self, out, in_):
        return self.do(lambda e: e.tensor_copy(out, in_))

    def tt(self, out, a, b, op, apart=False):
        return self.do(lambda e: e.tensor_tensor(out, a, b, op), apart)

    def ts(self, out, a, s1, s2, op0, op1, apart=False):
        if s2 is None:
            return self.do(lambda e: e.tensor_scalar(out, a, s1, None, op0), apart)
        return self.do(lambda e: e.tensor_scalar(out, a, s1, s2, op0, op1), apart)

    def stt(self, out, a, s, b, op0, op1):
        return self.do(lambda e: e.scalar_tensor_tensor(out, a, s, b, op0, op1))

    def red(self, out, in_, op):
        return self.do(lambda e: e.tensor_reduce(out, in_, AX, op))

    def rec(self, out, in_):
        return self.do(lambda e: e.reciprocal(out, in_))

    def ms(self, out, v):
        return self.do(lambda e: e.memset(out, v))

    def scan(self, out, d0, d1, apart=False):
        return self.do(lambda e: e.tensor_tensor_scan(out, d0, d1, 0.0, ALU.mult, ALU.add), apart)


class Scalar(Lanes):
    def ac(self, out, in_, f, bias=0.0, scale=1.0, acc=None, apart=False):
        return self.do(lambda e: e.activation(out, in_, f, bias=bias, scale=scale, accum_out=acc), apart)

    def cp(self, out, in_, apart=False):
        return self.ac(out, in_, ACT.Copy, apart=apart)


class Lane:

    def __init__(self, sem):
        self.sem, self.n = sem, 0


class Bank:

    def __init__(self, ap):
        self.ap, self.free = ap, []


class Slot:

    def __init__(self, ap, lane):
        self.ap, self.lane, self.free, self.tok = ap, lane, [], None


LEVELS = [1, 2, 4, 8, 16, 32, 64]
TILES = 4
NEG = -1.0e30


def constants():
    i = np.arange(128)
    r, c = i[:, None], i[None, :]
    parts = {
        "ident": r == c, "le": r <= c, "gt": r > c, "ge": r >= c, "lt": r < c,
        "ones": np.ones((128, 128)), "iota": np.broadcast_to(c, (128, 128)),
        "par": np.stack([(i // 16) % 2 == 0, (i // 16) % 2 == 1, i < 64, i >= 64], 1),
        "sel": np.stack([np.broadcast_to(i == h, (128, 128)).T for h in range(8)], 1).reshape(128, 1024),
    }
    t = np.arange(256)
    parts["causal"] = np.concatenate([np.where(t[None, :] <= 128 * n + r, 0.0, NEG) for n in range(2)], 1)
    inv = 10000.0 ** (-np.arange(0, 64, 2, dtype=np.float32) / np.float32(64))
    ang = np.concatenate([(t // 64)[:, None] * inv, (t % 64)[:, None] * inv], 1).astype(np.float32)
    for name, f in (("cos", np.cos), ("sin", np.sin)):
        parts[name] = f(ang).reshape(2, 128, 64).transpose(1, 0, 2).reshape(128, 128)
    lev = []
    for s in LEVELS:
        m = (r // (2 * s) == c // (2 * s)) & ((r // s) % 2 == 1) & ((c // s) % 2 == 0)
        lev += [m, m.T]
    parts["lev"] = np.concatenate(lev, 1)
    off, at = {}, 0
    for k, v in parts.items():
        off[k] = (at, v.shape[1])
        at += v.shape[1]
    return np.concatenate([np.asarray(v, np.float32) for v in parts.values()], 1), off


VECS = [("norm1_g", 0), ("norm1_g", 1), ("norm2_g", 0), ("norm2_g", 1), ("norm_mix_2", 0), ("norm_mix_2", 1),
        ("norm_ffn_2", 0), ("norm_ffn_2", 1), ("od_d_2", 0), ("c", 0), ("c_ctx", None)]


class Model:
    def __init__(self, nc, ins, out, ctx):
        self.nc, self.i, self.out, self.ctx = nc, ins, out, ctx
        self.nsem = 0
        self.P = Tensor("pe", self.sem)
        self.V = Lanes("dve", self.sem)
        self.S = Scalar("act", self.sem)
        self.G = Lanes("pool", self.sem)
        self.SP = Engine("sp", self.sem)
        self.psum = ctx.enter_context(nc.psum_tensor("psum", [128, 8, 512], F32))
        self.banks = [Bank(self.psum[:, b, :]) for b in range(8)]
        self.X = self.tensor("x_res", 4 * 1024).rearrange("p (t d) -> p t d", t=4)
        self.ring = [Slot(self.tensor(f"ring{n}", 2048), Lane(self.sem(f"l_ring{n}"))) for n in range(3)]
        self.nring = 0
        self.cv, self.off = None, None
        self.mod = self.tensor("mod", 2 * 4 * 8 * 2).rearrange("p (l k c v) -> p l k c v", l=2, k=4, c=8)
        self.vc = self.tensor("vc", 128)
        self.small = self.tensor("small", 64)
        self.arena_n = 41500
        self.arena = self.tensor("arena", self.arena_n)
        self.top = 0
        self.flip = 0
        self.tables = None
        self.stores = []

    def sem(self, name):
        self.nsem += 1
        return self.ctx.enter_context(self.nc.semaphore(name))

    def tensor(self, name, n, dt=F32):
        return self.ctx.enter_context(self.nc.sbuf_tensor(name, [128, n], dt))[:, :]

    def al(self, n, shape=None, names=None):
        a = self.arena[:, self.top:self.top + n]
        self.top += n
        assert self.top <= self.arena_n, self.top
        return a

    def al2(self, a, b):
        return self.al(a * b).rearrange("p (a b) -> p a b", a=a)

    def al3(self, a, b, c):
        return self.al(a * b * c).rearrange("p (a b c) -> p a b c", a=a, b=b)

    def stage(self):
        engines = [self.P, self.V, self.S, self.G]
        ends = [self.P.done(), self.V.last, self.S.last, self.G.last]
        for e in engines:
            e.wait(ends, self.stores)
        self.stores = []
        self.top = 0

    def const(self, name, a=0, n=None):
        o, w = self.off[name]
        return self.cv[:, o + a:o + (w if n is None else a + n)]

    def either(self):
        self.flip ^= 1
        return self.V if self.flip else self.S

    def misc(self, out, in_):
        return self.G.dma(Lane(self.sem(f"l_m{self.nsem}")), out, in_)

    def load(self, pieces):
        s = self.ring[self.nring % len(self.ring)]
        self.nring += 1
        self.SP.wait(s.free)
        for dst, src in pieces:
            s.tok = self.SP.dma(s.lane, dst(s.ap), src)
        s.free = None
        return s

    def rstd(self, out, ss, n, ready):
        self.V.wait(ready)
        t = self.V.ts(out, ss, 1.0 / n, 1e-06, ALU.mult, ALU.add)
        self.S.wait(t)
        t = self.S.ac(out, out, ACT.Sqrt)
        self.V.wait(t)
        return self.V.rec(out, out)

    def wslot(self, W, k0, nk, n0, nw):
        src = W[k0 * 128:(k0 + nk) * 128, n0:n0 + nw].rearrange("(k p) n -> p k n", p=128)
        s = self.load([(lambda a: a[:, 0:nk * nw].rearrange("p (k n) -> p k n", k=nk), src)])
        return s, s.ap[:, 0:nk * nw].rearrange("p (k n) -> p k n", k=nk)

    def proj_tok(self, hT, KC, W, N, ntile, cb, dep, banks=None, base=0):
        banks = banks or self.banks
        turn = 0
        self.P.wait(dep)
        for n0 in range(0, N, 512):
            nw = min(512, N - n0)
            bs = [banks[(turn + t) % len(banks)] for t in range(ntile)]
            turn += ntile
            for k0 in range(0, KC, 4):
                nk = min(4, KC - k0)
                s, w = self.wslot(W, k0, nk, base + n0, nw)
                self.P.wait(s.tok)
                for t in range(ntile):
                    self.P.wait(bs[t].free)
                    for k in range(nk):
                        self.P.mm(bs[t].ap[:, 0:nw], hT[:, k0 + k, t * 128:(t + 1) * 128], w[:, k, :], k0 + k == 0,
                                  k0 + k == KC - 1)
                    tk = self.P.done()
                    bs[t].done = tk
                s.free = [tk]
            for t in range(ntile):
                bs[t].free = [cb(t, n0, nw, bs[t].ap, bs[t].done)]

    def proj_feat(self, hT, KC, W, N, nt, cb, dep, banks=None, base=0):
        banks = banks or self.banks
        self.P.wait(dep)
        for n0 in range(0, N, 256):
            s, w = self.wslot(W, 0, KC, base + n0, 256)
            self.P.wait(s.tok)
            for j in range(2):
                b = banks[(n0 // 128 + j) % len(banks)]
                self.P.wait(b.free)
                for k in range(KC):
                    self.P.mm(b.ap[:, 0:nt], w[:, k, j * 128:(j + 1) * 128], hT[:, k, 0:nt], k == 0, k == KC - 1)
                tk = self.P.done()
                s.free = [tk]
                b.free = [cb(n0 // 128 + j, b.ap, tk)]

    def norm_T(self, tiles, hT, A, B, scr, dep=None, banks=None):
        banks = banks or self.banks[0:4]
        sq, st = scr[:, 0:1024], scr[:, 2048:2056]
        last = [None, None]
        self.S.wait(dep)
        for n, t in enumerate(tiles):
            z = self.S.ac(sq, self.X[:, t, :], ACT.Square, acc=st[:, n:n + 1])
        z = self.rstd(st[:, 0:len(tiles)], st[:, 0:len(tiles)], 1024, z)
        for n, t in enumerate(tiles):
            a, b = A[n], B[n] if B is not None else None
            xn = scr[:, 1024:2048] if n % 2 == 0 else scr[:, 2056:3080]
            free = self.xn_free[n % 2] if n >= 2 else None
            self.V.wait(z, free)
            z = self.V.ts(xn, self.X[:, t, :], st[:, n:n + 1], None, ALU.mult, None)
            self.P.wait(z)
            for half in range(2):
                bk = banks[(2 * n + half) % len(banks)]
                self.P.wait(bk.free)
                for k in range(4):
                    self.P.tr(bk.ap[:, k * 128:(k + 1) * 128], xn[:, (half * 4 + k) * 128:(half * 4 + k + 1) * 128])
                tk = self.P.done()
                for k in range(4):
                    c = half * 4 + k
                    o, i = hT[:, c, n * 128:(n + 1) * 128], bk.ap[:, k * 128:(k + 1) * 128]
                    if half == 0:
                        self.S.wait(tk)
                        f = self.S.ac(o, i, ACT.Identity, scale=a[:, c:c + 1], bias=b[:, c:c + 1] if b is not None else 0.0)
                    elif b is not None:
                        self.V.wait(tk)
                        f = self.V.ts(o, i, a[:, c:c + 1], b[:, c:c + 1], ALU.mult, ALU.add)
                    else:
                        self.V.wait(tk)
                        f = self.V.ts(o, i, a[:, c:c + 1], None, ALU.mult, None)
                bk.free = [f]
                last[half] = f
            self.xn_free[n % 2] = tk
        return last

    def to_T(self, src, n, dst, dep, banks=None):
        banks = banks or self.banks[0:4]
        toks = []
        self.P.wait(dep)
        for c0 in range(0, n, 4):
            m = min(4, n - c0)
            bk = banks[(c0 // 4) % len(banks)]
            self.P.wait(bk.free)
            for k in range(m):
                self.P.tr(bk.ap[:, k * 128:(k + 1) * 128], src[:, (c0 + k) * 128:(c0 + k + 1) * 128])
            tk = self.P.done()
            q = self.either()
            q.wait(tk)
            f = q.cp(dst[:, c0:c0 + m, :], bk.ap[:, 0:m * 128].rearrange("p (k n) -> p k n", k=m))
            bk.free = [f]
            toks.append(f)
        return toks[-2:]

    def begin(self):
        self.xn_free = [None, None]
        consts, self.off = constants()
        self.nconst = self.off["par"][0] + 4
        self.cv = self.tensor("consts", self.nconst)
        c_d = self.i["consts"]
        t = self.misc(self.cv, c_d[:, 0:self.nconst])
        self.ident = self.P.ident = self.const("ident")
        self.V.wait(t)
        z = self.V.ms(self.small, 0.0)
        for n, (name, d) in enumerate((("ctx", 0), ("x", 2))):
            self.xtok = self.misc(self.X[:, d:d + 2, :], self.i[name][0].rearrange("(t p) d -> p t d", p=128))
            self.V.wait(self.xtok)
            self.small_t = self.V.cp(self.small[:, n:n + 1], self.X[:, d, 0:1])
        rows = self.al(128)
        lane = Lane(self.sem("l_vec"))
        for n, (name, l) in enumerate(VECS):
            src = self.i[name] if l is None else self.i[name][l]
            t = self.G.dma(lane, rows[8 * n:8 * n + 8, :], src.rearrange("(k p) -> k p", p=128))
        t = self.G.dma(lane, rows[88:89, :], self.i["dn_norm_g"])
        t = self.G.dma(lane, rows[89:93, :], self.i["ev_b_spatial_2"][0])
        b = self.banks[0]
        self.P.wait(t, z, b.free)
        self.P.tr(b.ap[:, 0:93], rows[0:93, :])
        tk = self.P.done()
        self.V.wait(tk)
        self.vtok = self.V.cp(self.vc[:, 0:93], b.ap[:, 0:93])
        b.free = [self.vtok]
        self.P.wait(self.vtok, self.xtok)
        self.S.wait(self.vtok)
        self.G.wait(self.vtok)

    def vec(self, name, l):
        n = 8 * VECS.index((name, l))
        return self.vc[:, n:n + 8]

    def ada(self):
        self.stage()
        cond = self.al2(8, 2)
        t = None
        for v, name in enumerate((("c", 0), ("c_ctx", None))):
            t = self.S.ac(cond[:, :, v], self.vec(*name), ACT.Silu)
        rows = [self.al(6144), self.al(6144)]
        bias = [self.al(6144), self.al(6144)]
        self.gates_d = self.nc.dram_tensor("gates_d", [2, 2, 2, 1024], F32, kind="Internal").ap()
        self.gtok = {}
        self.P.wait(t)
        for l in range(2):
            bt = self.misc(bias[l][0:2, :], self.i["ada_b"][l].partition_broadcast(2))
            last = None
            self.V.wait(bt)
            for n in range(12):
                b = self.banks[n % 4]
                self.P.wait(b.free)
                for k0 in (0, 4):
                    s, w = self.wslot(self.i["ada_w"][l], k0, 4, n * 512, 512)
                    self.P.wait(s.tok)
                    for k in range(4):
                        self.P.mm(b.ap[0:2, :], cond[:, k0 + k, :], w[:, k, :], k0 + k == 0, k0 + k == 7)
                    tk = self.P.done()
                    s.free = [tk]
                self.V.wait(tk)
                last = self.V.tt(rows[l][0:2, n * 512:(n + 1) * 512], b.ap[0:2, :], bias[l][0:2, n * 512:(n + 1) * 512],
                                 ALU.add)
                b.free = [last]
            self.G.wait(last)
            for w_, o in enumerate((2048, 5120)):
                self.gtok[l, w_] = self.misc(self.gates_d[l, w_], rows[l][0:2, o:o + 1024])
                self.stores.append(self.gtok[l, w_])
            b = self.banks[4 + l]
            self.P.wait(last, b.free)
            for kind, o in enumerate((0, 1024, 3072, 4096)):
                for c in range(8):
                    q = (kind * 8 + c) * 2
                    self.P.tr(b.ap[:, q:q + 2], rows[l][0:2, o + c * 128:o + (c + 1) * 128])
            tk = self.P.done()
            m = self.mod[:, l]
            self.V.wait(tk)
            z = self.V.cp(m, b.ap[:, 0:64].rearrange("p (k c v) -> p k c v", k=4, c=8))
            b.free = [z]
            for kind, name in ((1, "norm1_g"), (3, "norm2_g")):
                for v in range(2):
                    self.mtok = self.V.stt(m[:, kind, :, v], m[:, kind, :, v], 1.0, self.vec(name, l), ALU.add, ALU.mult)
        for q in (self.S, self.P, self.G):
            q.wait(self.mtok)

    def gate_rows(self, l, which, v, place, ready=None):
        self.G.wait(self.gtok[l, which], ready)
        return (place, self.misc(place, self.gates_d[l, which, v].partition_broadcast(128)))

    def mod_cols(self, l, which, tiles):
        vs = [1 if t < 2 else 0 for t in tiles]
        return ([self.mod[:, l, 2 * which + 1, :, v] for v in vs], [self.mod[:, l, 2 * which, :, v] for v in vs])

    def add_gated(self, l, which, t, n0, nw, bank, tk, scr, gate):
        rows, got = gate[t // 2 if len(gate) > 1 else 0]
        self.V.wait(tk, got)
        z = self.V.tt(scr[:, 0:nw], bank[:, 0:nw], rows[:, n0:n0 + nw], ALU.mult)
        x = self.X[:, t, n0:n0 + nw]
        self.V.wait(z)
        self.V.tt(x, x, scr[:, 0:nw], ALU.add)
        return z

    def deltanet(self):
        self.stage()
        nc = self.nc
        W = self.i["dn_w_in"][0]
        hT = self.al2(8, 512)
        qT, kT, kt = self.al2(4, 512), self.al2(4, 512), self.al3(4, 4, 128)
        vt = self.al3(4, 8, 128)
        O = self.al3(4, 8, 128)
        lev = self.al(14 * 64).bitcast(BF16).rearrange("p (l m) -> p l m", l=14)
        cw = self.al2(32, 5)
        al, be, g = (self.al3(4, 2, 16) for _ in range(3))
        egc, erl, beg, egl = (self.al3(4, 2, 16) for _ in range(4))
        gates = self.al3(4, 2, 32)
        ssq, ssk = self.al2(4, 4), self.al2(4, 4)
        work = self.top
        scr = self.al(3080)
        A, B = self.mod_cols(0, 0, range(4))
        ht = self.norm_T(range(4), hT, A, B, scr)
        o = self.off["lev"][0]
        self.top = work + 3080
        tmp = self.al(14 * 128)
        t = self.misc(tmp, self.i["consts"][:, o:o + 14 * 128])
        self.V.wait(t)
        self.V.cp(lev, tmp.rearrange("p (l m) -> p l m", l=14))
        cr = self.al(4096)
        t = self.misc(cr[0:5, :], self.i["dn_conv_w"][0])
        b = self.banks[7]
        self.P.wait(t, b.free)
        for c in range(32):
            self.P.tr(b.ap[:, c * 5:c * 5 + 5], cr[0:5, c * 128:(c + 1) * 128])
        tk = self.P.done()
        self.V.wait(tk)
        z = self.V.cp(cw, b.ap[:, 0:160].rearrange("p (a b) -> p a b", a=32))
        b.free = [z]
        def gate_cols(t, n0, nw, bank, tk):
            self.V.wait(tk)
            return self.V.cp(gates[:, t], bank[:, 0:64].rearrange("p (d x) -> p d x", d=2))

        self.proj_tok(hT, 8, W, 64, 4, gate_cols, ht, base=6144)
        rows = self.al2(2, 32)
        lane = Lane(self.sem("l_alog"))
        self.G.dma(lane, rows[:, 0, :], self.i["dn_a_log"][0].rearrange("a b -> (a b)").partition_broadcast(128))
        t = self.G.dma(lane, rows[:, 1, :], self.i["dn_dt_bias"][0].rearrange("a b -> (a b)").partition_broadcast(128))
        r4 = [rows[:, n, :].rearrange("p (d h) -> p d h", d=2) for n in range(2)]
        self.S.wait(t)
        z = self.S.ac(rows[:, 0, :], rows[:, 0, :], ACT.Exp)
        sp = self.al3(4, 2, 16)
        for n in range(4):
            self.V.wait(z)
            z = self.V.tt(g[:, n], gates[:, n, :, 16:32], r4[1], ALU.add)
        self.S.wait(z)
        z = self.S.ac(sp, g, ACT.Abs)
        z = self.S.ac(sp, sp, ACT.Exp, scale=-1.0)
        self.V.wait(z)
        z = self.V.ts(sp, sp, 1.0, None, ALU.add, None)
        self.S.wait(z)
        z = self.S.ac(sp, sp, ACT.Ln)
        self.V.wait(z)
        z = self.V.stt(g, g, 0.0, sp, ALU.max, ALU.add)
        for n in range(4):
            self.V.wait(z)
            z = self.V.stt(g[:, n], g[:, n], -1.0, r4[0], ALU.mult, ALU.mult)
        self.S.wait(z)
        for n in range(4):
            bt = self.S.ac(be[:, n], gates[:, n, :, 0:16], ACT.Sigmoid)
        gated = z

        def sums(z):
            b = self.banks[6]
            self.P.wait(z, b.free)
            for n in range(4):
                for d in range(2):
                    r = g[:, n, d, :]
                    for w, m in enumerate((("le", "ge")[d], ("gt", "lt")[d], "ones")):
                        q = ((n * 2 + d) * 3 + w) * 16
                        self.P.mm(b.ap[:, q:q + 16], self.const(m), r, True, True)
            tk = self.P.done()
            bv = b.ap[:, 0:384].rearrange("p (n d w h) -> p n d w h", n=4, d=2, w=3)
            self.S.wait(tk)
            for n in range(4):
                for w, dst in enumerate((egc, erl, egl)):
                    z = self.S.ac(dst[:, n], bv[:, n, :, w, :], ACT.Exp)
            b.free = [z]
            self.V.wait(z, bt)
            gt_ = self.V.tt(beg, be, egc, ALU.mult)

        gs = None
        self.P.wait(ht)
        for half in range(2):
            if half:
                self.stage()
                self.top = work
            scr = self.al(512)
            pads = [self.al(520).rearrange("p (s t) -> p s t", s=2) for _ in range(2)]
            cvs = [self.al(512) for _ in range(2)]
            sqs = self.al(128)
            for p in pads:
                z = self.V.ms(p, 0.0)
            pfree, cfree = [z, z], [None, None]
            kb = self.banks[4:8]

            def conv(j, kind, c, n, bank, tk):
                p, cv_ = pads[j % 2], cvs[j % 2]
                self.S.wait(tk, pfree[j % 2])
                evac = self.S.ac(p[:, :, 2:258], bank.ap.rearrange("p (s t) -> p s t", s=2), ACT.Copy)
                bank.free = [evac]
                acc = cv_.rearrange("p (s t) -> p s t", s=2)
                self.V.wait(evac, cfree[j % 2])
                z = self.V.ts(acc, p[:, :, 0:256], cw[:, c, 0:1], None, ALU.mult, None)
                for w in range(1, 5):
                    z = self.V.stt(acc, p[:, :, w:w + 256], cw[:, c, w:w + 1], acc, ALU.mult, ALU.add)
                pfree[j % 2] = z
                dst = qT[:, n, :] if kind == "q" else cv_
                self.S.wait(z)
                z = self.S.ac(dst, cv_, ACT.Silu)
                return dst, z

            def to_rows(j, kind, n, src, z):
                tb = kb[j % 4]
                self.P.wait(z, tb.free)
                for m in range(4):
                    self.P.tr(tb.ap[:, m * 128:(m + 1) * 128], src[:, m * 128:(m + 1) * 128])
                tk = self.P.done()
                cfree[j % 2] = tk
                self.S.wait(tk)
                if kind != "v":
                    ss = ssq if kind == "q" else ssk
                    for m in range(4):
                        f = self.S.ac(sqs, tb.ap[:, m * 128:(m + 1) * 128], ACT.Square, acc=ss[:, m, n:n + 1])
                if kind != "q":
                    dst = kt if kind == "k" else vt
                    f = self.S.cp(dst[:, :, n, :], tb.ap.rearrange("p (t d) -> p t d", t=4))
                tb.free = [f]
                return f

            jobs = [("q", half * 4 + n, n) for n in range(4)] + [("k", 8 + half * 4 + n, n) for n in range(4)] + \
                   [("v", 16 + half * 8 + n, n) for n in range(8)]
            due = None
            for j in range(16):
                kind, c, n = jobs[j]
                if j % 2 == 0:
                    s, w = self.wslot(W, 0, 8, c * 128, 256)
                b = self.banks[j % 4]
                self.P.wait(s.tok, b.free)
                for k in range(8):
                    self.P.mm(b.ap, w[:, k, j % 2 * 128:(j % 2 + 1) * 128], hT[:, k, :], k == 0, k == 7)
                tk = self.P.done()
                s.free = [tk]
                if due:
                    to_rows(*due)
                if half == 0 and j == 8:
                    sums(gated)
                due = (j, kind, n, *conv(j, kind, c, n, b, tk))
            z = to_rows(*due)
            for ss in (ssq, ssk):
                self.V.wait(z)
                z = self.V.ts(ss, ss, 1e-06, None, ALU.add, None)
                self.S.wait(z)
                z = self.S.ac(ss, ss, ACT.Sqrt)
                self.V.wait(z)
                z = self.V.rec(ss, ss)
            z = self.V.ts(ssq, ssq, float(128 ** (-0.5)), None, ALU.mult, None)
            for m in range(4):
                z = self.V.tt(kt[:, m], kt[:, m], ssk[:, m, :].unsqueeze(2).to_broadcast([128, 4, 128]), ALU.mult)
            self.P.wait(z)
            for n in range(4):
                tb = kb[n]
                self.P.wait(tb.free)
                for m in range(4):
                    self.P.tr(tb.ap[:, m * 128:(m + 1) * 128], kt[:, m, n, :])
                tk = self.P.done()
                q = self.either()
                q.wait(tk)
                f = q.cp(kT[:, n, :], tb.ap)
                tb.free = [f]
            self.stage()
            self.top = work
            seen = set()
            chains = [self.chain(half, hg, d, [self.banks[2 * (hg * 2 + d)], self.banks[2 * (hg * 2 + d) + 1]],
                                 qT, kT, kt, vt, O, lev, g, be, egc, erl, beg, egl, seen)
                      for hg in range(2) for d in range(2)]
            while chains:
                live = []
                for ch in chains:
                    if next(ch, None) is not None:
                        live.append(ch)
                chains = live
            self.stage()
            self.top = work
            zs = self.al(1024)
            oT = self.al2(8, 512)
            sq = self.al3(1, 8, 128)[:, 0]
            st = self.al2(4, 8)
            scr = self.al(512)
            for t in range(4):
                for n in range(8):
                    z = self.V.ts(O[:, t, n, :], O[:, t, n, :], ssq[:, t, n // 2:n // 2 + 1], None, ALU.mult, None)
                z = self.V.tt(sq, O[:, t], O[:, t], ALU.mult)
                z = self.V.red(st[:, t, :], sq, ALU.add)
            z = self.rstd(st, st, 128, z)
            for t in range(4):
                z = self.V.tt(O[:, t], O[:, t], st[:, t, :].unsqueeze(2).to_broadcast([128, 8, 128]), ALU.mult)
            self.zf = [None, None]

            def zgate(t, n0, nw, bank, tk):
                q = (n0 // 512 * 4 + t) % 2
                self.S.wait(tk, self.zf[q])
                zz = self.S.ac(zs[:, q * 512:q * 512 + 512], bank, ACT.Silu)
                ov = O[:, t].rearrange("p h d -> p (h d)")[:, n0:n0 + 512]
                self.V.wait(zz)
                self.zf[q] = self.V.tt(ov, ov, zs[:, q * 512:q * 512 + 512], ALU.mult)
                return zz

            self.proj_tok(hT, 8, W, 1024, 4, zgate, ht, base=4096 + half * 1024)
            self.P.wait(self.zf[0], self.zf[1])
            for t in range(4):
                for h0 in (0, 4):
                    tb = self.banks[(t * 2 + h0 // 4) % 8]
                    self.P.wait(tb.free)
                    for h in range(4):
                        self.P.tr(tb.ap[:, h * 128:(h + 1) * 128], O[:, t, h0 + h, :])
                    tk = self.P.done()
                    q = self.either()
                    dst = oT[:, h0:h0 + 4, t * 128:(t + 1) * 128]
                    srcv = tb.ap.rearrange("p (h n) -> p h n", h=4)
                    if q is self.S:
                        self.S.wait(tk)
                        f = self.S.ac(dst, srcv, ACT.Copy, scale=self.ng)
                    else:
                        self.V.wait(tk)
                        f = self.V.ts(dst, srcv, self.ng, None, ALU.mult, None)
                    tb.free = [f]
            ot = [self.S.last, self.V.last]
            gs = [self.gate_rows(0, 0, v, self.al(1024), self.V.last) for v in (1, 0)]
            Wo = self.i["dn_w_out"][0]
            bs = self.banks
            self.P.wait(ot)
            for k0 in range(0, 8, 2):
                s, w = self.wslot(Wo, half * 8 + k0, 2, 0, 1024)
                self.P.wait(s.tok)
                for t in range(4):
                    for nh in range(2):
                        bk = bs[t * 2 + nh]
                        self.P.wait(bk.free)
                        for k in range(2):
                            self.P.mm(bk.ap, oT[:, k0 + k, t * 128:(t + 1) * 128], w[:, k, nh * 512:(nh + 1) * 512],
                                      k0 + k == 0, k0 + k == 7)
                        tk = self.P.done()
                        bk.done = tk
                s.free = [tk]
            for t in range(4):
                for nh in range(2):
                    bk = bs[t * 2 + nh]
                    bk.free = [self.add_gated(0, 0, t, nh * 512, 512, bk.ap, bk.done, scr, gs)]

    def chain(self, half, hg, d, bk, qT, kT, kt, vt, O, lev, g, be, egc, erl, beg, egl, seen):
        bufs = [self.al3(1, 4, 128)[:, 0] for _ in range(8)]
        gL, D, DT, T, Pm, Xp, M1, S = bufs
        h0 = half * 8 + hg * 4
        le, gt, ge, lt = (self.const(n) for n in (("le", "gt", "ge", "lt") if d == 0 else ("ge", "lt", "le", "gt")))
        b0, b1 = bk
        v4 = lambda b: b.ap.rearrange("p (h n) -> p h n", h=4)
        pair = lambda a: a.rearrange("p (h n) -> p h n", h=2).unsqueeze(2).to_broadcast([128, 2, 2, 128])
        four = lambda a: a.rearrange("p (h r) n -> p h r n", h=2)
        rep = lambda a: a.unsqueeze(1).to_broadcast([128, 4, 128])
        V, Sc, G = self.V, self.S, self.G
        first = True
        sfree = None
        for n in ((0, 1, 2, 3) if d == 0 else (1, 0, 3, 2)):
            tok = slice(n * 128, (n + 1) * 128)
            col = lambda a: a[:, n, d, h0:h0 + 4].unsqueeze(2).to_broadcast([128, 4, 128])
            V.wait(b0.free)
            z1 = V.tt(gL, rep(gt), col(g), ALU.mult, apart=True)
            yield 1
            self.P.wait(z1, b0.free)
            self.P.mm(b0.ap, le, gL.rearrange("p h n -> p (h n)"), True, True)
            t0 = self.P.done()
            self.P.wait(z1, b1.free)
            for h in range(4):
                self.P.mm(b1.ap[:, h * 128:(h + 1) * 128], gL[:, h, :], le, True, True)
            t1 = self.P.done()
            yield 1
            self.S.wait(t0)
            a0 = self.S.ac(D, v4(b0), ACT.Exp, apart=True)
            self.S.wait(t1)
            a1 = self.S.ac(DT, v4(b1), ACT.Exp, apart=True)
            G.wait(t1, sfree)
            z1 = G.tt(M1, rep(gt), col(be), ALU.mult, apart=True)
            yield 1
            self.P.wait(a0)
            for q in range(2):
                kq = kT[:, hg * 2 + q, tok]
                self.P.mm(b0.ap[:, q * 128:(q + 1) * 128], kq, kq, True, True)
            t0 = self.P.done()
            self.P.wait(a1)
            for q in range(2):
                self.P.mm(b1.ap[:, q * 128:(q + 1) * 128], kT[:, hg * 2 + q, tok], qT[:, hg * 2 + q, tok], True, True)
            t1 = self.P.done()
            V.wait(a0, z1)
            z = V.tt(D, D, M1, ALU.mult, apart=True)
            V.wait(a1)
            z2 = V.tt(DT, DT, rep(le), ALU.mult, apart=True)
            yield 1
            V.wait(t0, z)
            z = V.tt(four(D), four(D), pair(b0.ap[:, 0:256]), ALU.mult, apart=True)
            V.wait(t1, z2)
            z2 = V.tt(four(DT), four(DT), pair(b1.ap[:, 0:256]), ALU.mult, apart=True)
            b0.free, b1.free = [z], [z2]
            G.wait(z, z2)
            zc = G.tt(gL, D, rep(lev[:, d, :]), ALU.mult, apart=True)
            yield 1
            self.P.wait(zc, b0.free)
            for h in range(4):
                self.P.tr(b0.ap[:, h * 128:(h + 1) * 128], gL[:, h, :])
            t0 = self.P.done()
            yield 1
            V.wait(zc)
            zt = V.tt(T, rep(self.ident), gL, ALU.subtract, apart=True)
            V.wait(t0)
            zp = V.tt(Pm, rep(self.ident), v4(b0), ALU.subtract, apart=True)
            b0.free = [zp]
            G.wait(t0, zt)
            zc = G.tt(gL, D, rep(lev[:, 2 + d, :]), ALU.mult, apart=True)
            yield 1
            for l in range(1, 7):
                self.P.wait(zc, zp, b0.free)
                for h in range(4):
                    self.P.mm(b0.ap[:, h * 128:(h + 1) * 128], gL[:, h, :], Pm[:, h, :], True, True)
                t0 = self.P.done()
                yield 1
                Sc.wait(t0)
                zx = Sc.cp(Xp, v4(b0), apart=True)
                b0.free = [zx]
                if l < 6:
                    G.wait(t0)
                    zc = G.tt(gL, D, rep(lev[:, 2 * l + 2 + d, :]), ALU.mult, apart=True)
                yield 1
                self.P.wait(zx, zt, b1.free)
                for h in range(4):
                    self.P.mm(b1.ap[:, h * 128:(h + 1) * 128], T[:, h, :], Xp[:, h, :], True, True)
                t1 = self.P.done()
                yield 1
                V.wait(t1)
                zp = V.tt(Pm, Pm, v4(b1), ALU.subtract, apart=True)
                b1.free = [zp]
                yield 1
                if l < 6:
                    self.P.wait(zp, b0.free)
                    for h in range(4):
                        self.P.tr(b0.ap[:, h * 128:(h + 1) * 128], Pm[:, h, :])
                    t0 = self.P.done()
                    yield 1
                    Sc.wait(t0)
                    zt = Sc.cp(T, v4(b0), apart=True)
                    b0.free = [zt]
            kv = kt[:, n, hg * 2:hg * 2 + 2, :].unsqueeze(2).to_broadcast([128, 2, 2, 128])
            G.wait(zp)
            zk = G.tt(four(M1), kv,
                      beg[:, n, d, h0:h0 + 4].rearrange("p (a b) -> p a b",
                                                        a=2).unsqueeze(3).to_broadcast([128, 2, 2, 128]), ALU.mult, apart=True)
            V.wait(zp)
            zv = V.tt(D, vt[:, n, hg * 4:hg * 4 + 4, :], col(be), ALU.mult, apart=True)
            yield 1
            if not first:
                self.P.wait(zk, zp, b0.free)
                for h in range(4):
                    self.P.mm(b0.ap[:, h * 128:(h + 1) * 128], M1[:, h, :], Pm[:, h, :], True, True)
                t0 = self.P.done()
                self.S.wait(t0)
                zx = self.S.ac(Xp, v4(b0), ACT.Copy, scale=-1.0, apart=True)
                b0.free = [zx]
                yield 1
            self.P.wait(zv, zp, b1.free)
            for h in range(4):
                o = b1.ap[:, h * 128:(h + 1) * 128]
                self.P.mm(o, Pm[:, h, :], D[:, h, :], True, first)
                if not first:
                    self.P.wait(zx, sfree)
                    self.P.mm(o, Xp[:, h, :], S[:, h, :], False, True)
            t1 = self.P.done()
            yield 1
            Sc.wait(t1)
            vn = Sc.cp(T, v4(b1), apart=True)
            b1.free = [vn]
            G.wait(t1, t0)
            zk = G.tt(four(M1), kv,
                      erl[:, n, d, h0:h0 + 4].rearrange("p (a b) -> p a b",
                                                        a=2).unsqueeze(3).to_broadcast([128, 2, 2, 128]), ALU.mult, apart=not first)
            yield 1
            if not first:
                self.P.wait(sfree, b0.free)
                for h in range(4):
                    self.P.mm(b0.ap[:, h * 128:(h + 1) * 128], qT[:, hg * 2 + h // 2, tok], S[:, h, :], True, True)
                t0 = self.P.done()
            self.P.wait(vn, z2, b1.free)
            for h in range(4):
                self.P.mm(b1.ap[:, h * 128:(h + 1) * 128], DT[:, h, :], T[:, h, :], True, True)
            t1 = self.P.done()
            Ov = O[:, n, hg * 4:hg * 4 + 4, :]
            yield 1
            fresh = (hg, n) not in seen
            seen.add((hg, n))
            if not first:
                V.wait(t0, t1)
                z = V.tt(gL, v4(b0), col(egc), ALU.mult, apart=True)
                b0.free = [z]
                if not fresh:
                    z = V.tt(Ov, Ov, gL, ALU.add)
                    V.wait(t1)
                    z = V.tt(Ov, Ov, v4(b1), ALU.add)
                else:
                    V.wait(t1)
                    z = V.tt(Ov, gL, v4(b1), ALU.add)
            elif fresh:
                V.wait(t1)
                z = V.cp(Ov, v4(b1))
            else:
                V.wait(t1)
                z = V.tt(Ov, Ov, v4(b1), ALU.add)
            b1.free = [z]
            yield 1
            self.P.wait(zk, vn, b0.free)
            for h in range(4):
                self.P.mm(b0.ap[:, h * 128:(h + 1) * 128], M1[:, h, :], T[:, h, :], True, True)
            t0 = self.P.done()
            yield 1
            if first:
                V.wait(t0)
                sfree = V.cp(S, v4(b0))
            else:
                V.wait(t0)
                z = V.tt(S, S, col(egl), ALU.mult, apart=True)
                sfree = V.tt(S, S, v4(b0), ALU.add)
            b0.free = [sfree]
            first = False
            yield 1

    def peer(self, l, tiles):
        self.stage()
        P, V, S, G = self.P, self.V, self.S, self.G
        C = self.al2(128, 256)
        pair = [[self.al(512).bitcast(BF16) for _ in range(2)] for _ in range(3)]
        hh = [self.al(1024).bitcast(BF16).rearrange("p (k n) -> p k n", k=8) for _ in range(2)]
        co = [[self.al(128).bitcast(BF16) for _ in range(2)] for _ in range(2)]
        half16 = lambda n: self.al(n // 2).bitcast(BF16)
        jT, iT, gT, iota16 = self.al(256), half16(256), [half16(256) for _ in range(2)], half16(128)
        eq = half16(512).rearrange("p (a n) -> p a n", a=8)
        hot = [[half16(8 * n).rearrange("p (a n) -> p a n", a=8) for n in (128, 64, 64)] for _ in range(2)]
        self.top = 64 * 256
        hT = self.al2(8, 256)
        skT = self.al2(16, 128)
        sc = self.al3(2, 16, 128)
        qs = [self.al(256) for _ in range(2)]
        mark = self.top
        scr = self.al(3080)
        A, B = self.mod_cols(l, 1, tiles)
        ht = self.norm_T(tiles, hT, A, B, scr)
        S.wait(ht)
        z = S.cp(hh[0], hT)
        V.wait(z)
        hp = V.tt(hh[1], hT, hh[0], ALU.subtract)
        sk = self.load([(lambda a: a.rearrange("p (h d) -> p h d", h=16),
                         self.i["peer_sub_keys"][l].rearrange("h c k d -> k (h c) d"))])
        skv = sk.ap.rearrange("p (h d) -> p h d", h=16)
        st = []
        P.wait(sk.tok)
        for c0 in range(0, 16, 4):
            b = self.banks[4 + (c0 // 4) % 4]
            P.wait(b.free)
            for k in range(4):
                P.tr(b.ap[:, k * 128:(k + 1) * 128], skv[:, c0 + k, :])
            tk = P.done()
            q = self.either()
            q.wait(tk)
            f = q.cp(skT[:, c0:c0 + 4, :], b.ap.rearrange("p (k n) -> p k n", k=4))
            b.free = [f]
            st.append(f)
        sk.free = [tk]
        qfree = [None, None]

        asked = []

        def query(c, bank, tk):
            S.wait(tk, qfree[c % 2])
            z = S.cp(qs[c % 2], bank[:, 0:256])
            if asked:
                score(*asked.pop())
            asked.append((c, z))
            return z

        def score(c, z):
            b = self.banks[4 + c % 4]
            P.wait(z, st, b.free)
            for t in range(2):
                P.mm(b.ap[:, t * 128:(t + 1) * 128], qs[c % 2][:, t * 128:(t + 1) * 128], skT[:, c, :], True, True)
            tk = P.done()
            qfree[c % 2] = tk
            V.wait(tk)
            b.free = [V.cp(sc[:, :, c, :], b.ap[:, 0:256].rearrange("p (t k) -> p t k", t=2))]

        self.proj_feat(hT, 8, self.i["peer_w_query"][l], 2048, 256, query, ht, banks=self.banks[0:4])
        score(*asked.pop())
        iota = self.const("iota")
        V.cp(iota16, iota)
        ub, ab, gb, yb = self.banks[0:2], self.banks[2:4], self.banks[4:8], self.banks[0:4]
        ug, vg = self.i["peer_u"][l], self.i["peer_v"][l]
        slots, split = {}, {}
        pfree, cfree, hfree = [None] * 3, [None] * 2, [None] * 2
        picked, made, weighed, due = [], {}, [None, None], []

        def fetch(kind, i):
            if i % 2 == 0:
                src = kind[i * 128:(i + 2) * 128, :].rearrange("(b p) d -> p b d", p=128)
                slots[0] = self.load([(lambda a: a.rearrange("p (b d) -> p b d", b=2), src)])
            s = slots[0]
            return s, s.ap[:, (i % 2) * 1024:(i % 2 + 1) * 1024]

        def take_u(i):
            s, rows = fetch(ug, i)
            hi, lo = (a.rearrange("p (k n) -> p k n", k=8) for a in pair[i % 3])
            split[i] = []
            for half in range(2):
                b = ub[half]
                P.wait(s.tok, b.free)
                for k in range(4):
                    c = half * 4 + k
                    P.tr(b.ap[:, k * 128:(k + 1) * 128], rows[:, c * 128:(c + 1) * 128])
                tk = P.done()
                bv = b.ap.rearrange("p (k n) -> p k n", k=4)
                sl = slice(half * 4, half * 4 + 4)
                S.wait(tk, pfree[i % 3])
                f = S.cp(hi[:, sl, :], bv, apart=True)
                V.wait(f)
                f = V.tt(lo[:, sl, :], bv, hi[:, sl, :], ALU.subtract, apart=True)
                b.free = [f]
                split[i].append(f)
            s.free = [tk]

        def gelu(i):
            b = ab[i % 2]
            hi, lo = (a.rearrange("p (k n) -> p k n", k=8) for a in pair[i % 3])
            P.wait(split[i], hp, b.free)
            for k in range(8):
                for n, (x, y) in enumerate(((hi, hh[0]), (hi, hh[1]), (lo, hh[0]))):
                    P.mm(b.ap[:, 0:256], x[:, k, :], y[:, k, :], k == 0 and n == 0, k == 7 and n == 2)
            tk = P.done()
            pfree[i % 3] = tk
            S.wait(tk)
            if i >= 64:
                S.wait(picked)
            f = S.ac(C[:, i, :], b.ap[:, 0:256], ACT.Gelu, apart=True)
            b.free = [f]
            return f

        def rows_of_weights(half, m):
            bj, ahi, alo = hot[m % 2]
            G.wait(picked, hfree[m % 2])
            for n in range(8):
                zg = G.ts(bj[:, n, :], iota, jT[:, 8 * m + n:8 * m + n + 1], None, ALU.is_equal, None, apart=True)
            cols = slice(8 * m, 8 * m + 8)
            wide = lambda a: a[:, cols].unsqueeze(2).to_broadcast([128, 8, 64])
            V.wait(picked, hfree[m % 2])
            V.tt(eq, iota16[:, 64 * half:64 * half + 64].unsqueeze(1).to_broadcast([128, 8, 64]), wide(iT), ALU.is_equal)
            V.tt(ahi, eq, wide(gT[0]), ALU.mult)
            zv = V.tt(alo, eq, wide(gT[1]), ALU.mult, apart=True)
            made[m] = [zg, zv]

        def weights(half, m):
            bj, ahi, alo = hot[m % 2]
            b = gb[m % 4]
            P.wait(made[m], b.free)
            for n in range(8):
                P.mm(b.ap[:, n * 64:n * 64 + 64], bj[:, n, :], ahi[:, n, :], True, False)
                P.mm(b.ap[:, n * 64:n * 64 + 64], bj[:, n, :], alo[:, n, :], False, True)
            tk = P.done()
            hfree[m % 2] = tk
            due.append((half, m, tk))

        def weigh(ready):
            half, m, tk = due.pop()
            b = gb[m % 4]
            c = C[:, 64 * half:64 * half + 64, 8 * m:8 * m + 8]
            V.wait(tk, ready)
            f = V.tt(c, c, b.ap.rearrange("p (t i) -> p i t", t=8), ALU.mult, apart=True)
            b.free = [f]
            weighed[half] = f

        def take_v(i):
            s, rows = fetch(vg, i)
            hi, lo = pair[(i + 2) % 3]
            S.wait(s.tok, pfree[(i + 2) % 3])
            f = S.cp(hi, rows, apart=True)
            V.wait(f)
            split[i] = V.tt(lo, rows, hi, ALU.subtract, apart=True)
            s.free = [split[i]]

        def coefs(i):
            hi, lo = co[i % 2]
            S.wait(weighed[i // 64], cfree[i % 2])
            f = S.cp(hi, C[:, i, :], apart=True)
            V.wait(f)
            made["c", i] = V.tt(lo, C[:, i, :], hi, ALU.subtract, apart=True)

        def mix(i):
            chi, clo = co[i % 2]
            vhi, vlo = pair[(i + 2) % 3]
            P.wait(made["c", i], split[i])
            for t in range(2):
                ts_ = slice(t * 128, (t + 1) * 128)
                for n, (x, y) in enumerate(((chi, vhi), (chi, vlo), (clo, vhi))):
                    for nh in range(2):
                        P.mm(yb[t * 2 + nh].ap, x[:, ts_], y[:, nh * 512:(nh + 1) * 512],
                             i == 0 and n == 0, i == 127 and n == 2)
            cfree[i % 2] = pfree[(i + 2) % 3] = P.done()

        choice = self.choose(sc, mark, gb, iT, jT, gT, picked)
        take_u(0)
        for i in range(128):
            if i + 1 < 128:
                take_u(i + 1)
            last = gelu(i)
            if i < 63:
                next(choice, None)
            if i == 63:
                for _ in choice:
                    pass
                low = last
                rows_of_weights(0, 0)
            if i >= 64:
                m = (i - 64) // 2
                if due:
                    weigh(low)
                if i % 2 == 0 and m < 31:
                    rows_of_weights(0, m + 1)
                if i % 2:
                    weights(0, m)
        weigh(low)
        take_v(0)
        coefs(0)
        rows_of_weights(1, 0)
        for b in yb:
            P.wait(b.free)
        for i in range(128):
            if i % 2 == 0 and i < 62:
                rows_of_weights(1, i // 2 + 1)
            if i + 1 < 128:
                take_v(i + 1)
            if i == 63:
                weights(1, 31)
                weigh(last)
            if i + 1 < 128:
                coefs(i + 1)
            if due:
                weigh(last)
            if i % 2 and i < 63:
                weights(1, i // 2)
            mix(i)
            if i == 100:
                self.top = 0
                gs = [self.gate_rows(l, 1, 1 if tiles[0] < 2 else 0, self.al(1024), made["c", 8])]
                s2 = self.al(512)
        tk = P.done()
        for t in range(2):
            for nh in range(2):
                bk = yb[t * 2 + nh]
                bk.free = [self.add_gated(l, 1, tiles[t], nh * 512, 512, bk.ap, tk, s2, gs)]

    def choose(self, sc, mark, gb, iT, jT, gT, picked):
        P, V, S = self.P, self.V, self.S
        iota = self.const("iota")
        self.top = mark
        val, idx, idf = self.al2(16, 16), self.al2(16, 16).bitcast(U32), self.al2(16, 16)
        sw, cw = self.al2(16, 128), self.al2(8, 256)
        best, pos = self.al2(8, 16), self.al2(8, 16).bitcast(U32)
        nm, sm = self.al(8), self.al(8)
        pi, pf = self.al(128).bitcast(U32), self.al(128)
        out = self.al2(3, 128)
        part = self.al(64).bitcast(BF16)
        assert self.top <= 128 * 256
        cand = sw.rearrange("p c k -> p (c k)").rearrange("p (h a b) -> p h a b", h=8, a=16)
        eq = cw.rearrange("p h k -> p (h k)").rearrange("p (h k a) -> p h k a", h=8, k=16)
        vv = val.rearrange("p (h c) k -> p h c k", c=2)
        iv = idf.rearrange("p (h c) k -> p h c k", c=2)
        pv = pos.rearrange("p h k -> p (h k)")
        e3 = eq.rearrange("p h k a -> p (h k) a")
        tk = None
        for t in range(2):
            for c in range(16):
                self.top16(sc[:, t, c, :], sw[:, c, :], val[:, c, :], idx[:, c, :])
                yield
            V.cp(idf, idx)
            V.tt(cand, vv[:, :, 0, :].unsqueeze(3).to_broadcast([128, 8, 16, 16]),
                 vv[:, :, 1, :].unsqueeze(2).to_broadcast([128, 8, 16, 16]), ALU.add)
            yield
            for h in range(8):
                self.top16(cand[:, h].rearrange("p a b -> p (a b)"), cw[:, h, :], best[:, h, :], pos[:, h, :])
                yield
            V.cp(nm, best[:, :, 0])
            z = V.tt(best, best, nm.unsqueeze(2).to_broadcast([128, 8, 16]), ALU.subtract)
            S.wait(z)
            z = S.ac(best, best, ACT.Exp)
            V.wait(z)
            V.red(sm, best, ALU.add)
            V.rec(sm, sm)
            V.wait(tk)
            V.tt(out[:, 2, :].rearrange("p (h k) -> p h k", h=8), best, sm.unsqueeze(2).to_broadcast([128, 8, 16]), ALU.mult)
            yield
            for w in range(2):
                if w == 0:
                    V.ts(pi, pv, 4, None, ALU.logical_shift_right, None)
                else:
                    V.ts(pi, pv, 15, None, ALU.bitwise_and, None)
                V.cp(pf, pi)
                V.tt(e3, pf.unsqueeze(2).to_broadcast([128, 128, 16]),
                     iota[:, 0:16].unsqueeze(1).to_broadcast([128, 128, 16]), ALU.is_equal)
                yield
                V.tt(eq, eq, iv[:, :, w, :].unsqueeze(2).to_broadcast([128, 8, 16, 16]), ALU.mult)
                z = V.red(out[:, w, :], e3, ALU.add)
                yield
            b = gb[t]
            P.wait(z, b.free)
            for w in range(3):
                P.tr(b.ap[:, w * 128:(w + 1) * 128], out[:, w, :])
            tk = P.done()
            yield
            V.wait(tk)
            cols = slice(t * 128, (t + 1) * 128)
            for w, dst in enumerate((iT, jT)):
                V.cp(dst[:, cols], b.ap[:, w * 128:(w + 1) * 128])
            V.cp(part, b.ap[:, 256:384])
            V.cp(gT[0][:, cols], part)
            z = V.tt(gT[1][:, cols], b.ap[:, 256:384], part, ALU.subtract)
            b.free = [z]
        picked.append(z)

    def top16(self, src, wrk, val, idx):
        V = self.V
        V.do(lambda e: e.max(val[:, 0:8], src))
        V.do(lambda e: e.max_index(idx[:, 0:8], val[:, 0:8], src))
        V.do(lambda e: e.match_replace(wrk, val[:, 0:8], src, -3.0e38))
        V.do(lambda e: e.max(val[:, 8:16], wrk))
        return V.do(lambda e: e.max_index(idx[:, 8:16], val[:, 8:16], wrk))

    def row_norm(self, x, heads, hd, gain, scr, st, ready=None):
        self.V.wait(ready)
        z = self.V.tt(scr, x, x, ALU.mult)
        z = self.V.red(st, scr, ALU.add)
        z = self.rstd(st, st, hd, z)
        z = self.V.tt(x, x, st.unsqueeze(2).to_broadcast([128, heads, hd]), ALU.mult)
        if gain is not None:
            z = self.V.tt(x, x, gain, ALU.mult)
        return z

    def attend(self, scores, width, values, scale, put):
        P, V, S = self.P, self.V, self.S
        Ps, pTs = [self.al(512) for _ in range(2)], [self.al(512) for _ in range(2)]
        mx, sm = self.al(16), self.al(16)
        ex, tr, cp, av, inv = {}, {}, {}, {}, {}
        for step in range(18):
            n = step
            if n < 16:
                place, ready, bank = scores(n, ex)
                V.wait(ready)
                V.red(mx[:, n:n + 1], place, ALU.max)
                z = V.ts(mx[:, n:n + 1], mx[:, n:n + 1], -scale, None, ALU.mult, None)
                S.wait(z, tr.get(n - 2))
                ex[n] = S.ac(Ps[n % 2][:, 0:width(n)], place, ACT.Exp, bias=mx[:, n:n + 1], scale=scale, acc=sm[:, n:n + 1])
                if bank:
                    bank.free = [ex[n]]
            n = step - 1
            if 0 <= n < 16:
                pb, w = self.banks[2 + n % 2], width(n)
                P.wait(ex[n], pb.free)
                for c in range(w // 128):
                    P.tr(pb.ap[:, c * 128:(c + 1) * 128], Ps[n % 2][:, c * 128:(c + 1) * 128])
                tr[n] = P.done()
                S.wait(tr[n], av.get(n - 2))
                cp[n] = S.cp(pTs[n % 2][:, 0:w], pb.ap[:, 0:w])
                pb.free = [cp[n]]
                V.wait(ex[n])
                inv[n] = V.rec(sm[:, n:n + 1], sm[:, n:n + 1])
            n = step - 2
            if n >= 0:
                ob, dst, last = self.banks[4 + n % 4], put(n), width(n) // 128 - 1
                o = ob.ap[:, 0:dst.shape[1]]
                P.wait(cp[n], ob.free)
                for c in range(last + 1):
                    P.mm(o, pTs[n % 2][:, c * 128:(c + 1) * 128], values(n, c), c == 0, c == last)
                av[n] = P.done()
                V.wait(av[n], inv[n])
                f = V.ts(dst, o, sm[:, n:n + 1], None, ALU.mult, None)
                ob.free = [f]
        return f

    def attention(self):
        self.stage()
        W = self.i["att_w_in"][0]
        hT = self.al2(8, 512)
        scr = self.al(3080)
        A, B = self.mod_cols(1, 0, range(4))
        ht = self.norm_T(range(4), hT, A, B, scr)
        q, k, v = self.al2(2, 1024), self.al2(4, 256), self.al2(4, 256)
        gq, gk, cs = self.al(128), self.al(128), self.al(256)
        lane = Lane(self.sem("l_att"))
        self.G.dma(lane, gq, self.i["att_qn_g"][0].partition_broadcast(128))
        self.G.dma(lane, gk, self.i["att_kn_g"][0].partition_broadcast(128))
        o = self.off["cos"][0]
        lt = self.G.dma(lane, cs, self.i["consts"][:, o:o + 256])
        def qcols(t, n0, nw, b, tk):
            self.V.wait(tk)
            return self.V.cp(q[:, t, n0:n0 + nw], b)

        self.proj_tok(hT[:, :, 256:512], 8, W, 1024, 2, qcols, ht)

        st = self.al(8)
        sq = self.al(1024)
        tmp = [self.al(512) for _ in range(4)]
        rots = [self.al(1024) for _ in range(2)]
        qT, kT = self.al2(8, 256), self.al2(2, 512)
        turned = []

        def kv(t, n0, nw, b, tk):
            self.S.wait(tk)
            self.S.cp(k[:, t, :], b[:, 0:256])
            self.S.wait(tk)
            return self.S.cp(v[:, t, :], b[:, 256:512])

        def rope(x, heads, t, out, z):
            xv = x.rearrange("p (h i e) -> p h i e", h=heads, e=2)
            ov = out[:, 0:heads * 128].rearrange("p (h i e) -> p h i e", h=heads, e=2)
            c = cs[:, t * 64:(t + 1) * 64].unsqueeze(1).to_broadcast([128, heads, 64])
            s = cs[:, 128 + t * 64:128 + (t + 1) * 64].unsqueeze(1).to_broadcast([128, heads, 64])
            m = [a[:, 0:heads * 64].rearrange("p (h i) -> p h i", h=heads) for a in tmp]
            self.V.wait(z)
            self.V.tt(m[0], xv[:, :, :, 0], c, ALU.mult)
            self.V.tt(m[1], xv[:, :, :, 1], s, ALU.mult)
            self.V.tt(m[2], xv[:, :, :, 0], s, ALU.mult)
            self.V.tt(m[3], xv[:, :, :, 1], c, ALU.mult)
            self.V.tt(ov[:, :, :, 0], m[0], m[1], ALU.subtract)
            return self.V.tt(ov[:, :, :, 1], m[2], m[3], ALU.add)

        for t in range(2):
            xq = q[:, t, :].rearrange("p (h d) -> p h d", h=8)
            z = self.row_norm(xq, 8, 128, gq.unsqueeze(1).to_broadcast([128, 8, 128]),
                              sq.rearrange("p (h d) -> p h d", h=8), st, lt)
            turned.append(rope(q[:, t, :], 8, t, rots[t], z))
        self.proj_tok(hT, 8, W, 512, 4, kv, ht, base=1024)
        jt = [self.S.last, self.V.last]
        for t in range(2):
            self.to_T(rots[t], 8, qT[:, :, t * 128:(t + 1) * 128], turned[t])
        rf, z = self.P.done(), jt
        for t in range(4):
            xk = k[:, t, :].rearrange("p (h d) -> p h d", h=2)
            z = self.row_norm(xk, 2, 128, gk.unsqueeze(1).to_broadcast([128, 2, 128]),
                              sq[:, 0:256].rearrange("p (h d) -> p h d", h=2), st[:, 0:2], z)
            src = k[:, t, :]
            if t >= 2:
                src = rots[t - 2][:, 0:256]
                z = rope(k[:, t, :], 2, t - 2, src, rf)
            turned = self.to_T(src, 2, kT[:, :, t * 128:(t + 1) * 128], z)
        z = turned + [self.S.last, self.V.last]
        o = self.al2(2, 1024)
        self.P.wait(z, jt)

        def scores(n, ex):
            t, h = n // 8, n % 8
            b = self.banks[n % 2]
            self.P.wait(b.free)
            self.P.mm(b.ap, qT[:, h, t * 128:(t + 1) * 128], kT[:, h // 4, :], True, True)
            return b.ap, self.P.done(), b

        f = self.attend(scores, lambda n: 512, lambda n, c: v[:, c, n % 8 // 4 * 128:(n % 8 // 4 + 1) * 128],
                        float(128 ** -0.5), lambda n: o[:, n // 8, n % 8 * 128:(n % 8 + 1) * 128])
        oT = self.al2(8, 256)
        for t in range(2):
            z = self.to_T(o[:, t, :], 8, oT[:, :, t * 128:(t + 1) * 128], f)
        gs = [self.gate_rows(1, 0, 0, self.al(1024))]

        def out_cols(t, n0, nw, b, tk):
            return self.add_gated(1, 0, t + 2, n0, nw, b, tk, sq, gs)

        self.proj_tok(oT, 8, self.i["att_w_out"][0], 1024, 2, out_cols, z)

    def final_norm(self):
        self.stage()
        g = self.al(1024)
        sq = self.al(1024)
        st = self.al(2)
        lt = self.misc(g, self.i["final_g"].partition_broadcast(128))
        self.V.wait(lt)
        for t in range(2):
            x = self.X[:, t + 2, :]
            z = self.S.ac(sq, x, ACT.Square, acc=st[:, t:t + 1])
            z = self.rstd(st[:, t:t + 1], st[:, t:t + 1], 1024, z)
            self.V.wait(z)
            z = self.V.stt(x, x, st[:, t:t + 1], g, ALU.mult, ALU.mult)
        self.S.wait(z)
        self.P.wait(z)

    def gain_cols(self, name, l):
        a = self.vec(name, l)
        return [a, a]

    def even_mixer(self):
        self.stage()
        W = self.i["ev_w_in_2"][0]
        hT = self.al2(8, 256)
        scr = self.al(3080)
        ht = self.norm_T([2, 3], hT, self.gain_cols("norm_mix_2", 0), None, scr)
        u, va, q, k, vb = (self.al2(2, 512) for _ in range(5))
        f8 = self.al2(2, 8)
        vg, qg, kg, fb, ws = self.al(512), self.al(64), self.al(64), self.al(8), self.al2(4, 128)
        causal = self.al2(2, 256)
        lane = Lane(self.sem("l_ev"))
        for dst, src in ((vg, "ev_v_norm_2"), (qg, "ev_q_norm_2"), (kg, "ev_k_norm_2"), (fb, "ev_b_fgate_2")):
            self.G.dma(lane, dst, self.i[src][0].partition_broadcast(128))
        self.G.dma(lane, ws, self.i["ev_w_spatial_2"][0].rearrange("g t s -> t g s"))
        co = self.off["causal"][0]
        lt = self.G.dma(lane, causal, self.i["consts"][:, co:co + 512].rearrange("p (a b) -> p a b", a=2))
        dst = [u, va, q, k, vb]
        sq, st = self.al(512), self.al(8)
        v4, s8 = (sq.rearrange("p (h d) -> p h d", h=h) for h in (4, 8))
        gated, unit = {}, {}

        def cb(t, n0, nw, b, tk):
            n = n0 // 512
            if n < 2:
                self.S.wait(tk)
                f = gated[t] = self.S.ac(dst[n][:, t, :], b, ACT.Gelu_apprx_tanh)
            elif n < 5:
                self.V.wait(tk)
                f = self.V.cp(dst[n][:, t, :], b)
            else:
                self.V.wait(tk)
                f = self.V.cp(f8[:, t, :], b[:, 0:8])
            if n == 2:
                unit["v", t] = self.row_norm(va[:, t, :].rearrange("p (h d) -> p h d", h=4), 4, 128,
                                             vg.rearrange("p (h d) -> p h d", h=4), v4, st[:, 0:4], [gated[t], lt])
            if n in (3, 4):
                x, gn = ((q, qg), (k, kg))[n - 3]
                z = self.row_norm(x[:, t, :].rearrange("p (h d) -> p h d", h=8), 8, 64,
                                  gn.unsqueeze(1).to_broadcast([128, 8, 64]), s8, st, lt)
                if n == 3:
                    z = self.V.ts(x[:, t, :], x[:, t, :], 0.125, None, ALU.mult, None)
                unit[n, t] = z
            return f

        self.proj_tok(hT, 8, W, 2568, 2, cb, ht)
        jt = [self.S.last, self.V.last]
        y = self.al2(2, 1024)
        qT, kT = self.al2(4, 256), self.al2(4, 256)
        turned = []
        for n, x, xT in ((3, q, qT), (4, k, kT)):
            for t in range(2):
                turned += self.to_T(x[:, t, :], 4, xT[:, :, t * 128:(t + 1) * 128], unit[n, t])
        wT = self.al2(4, 128)
        b = self.banks[0]
        self.P.wait(lt, b.free)
        for g in range(4):
            self.P.tr(b.ap[:, g * 128:(g + 1) * 128], ws[:, g, :])
        tk = self.P.done()
        self.V.wait(tk)
        z = self.V.tt(wT, b.ap.rearrange("p (g t) -> p g t", g=4), self.const("le").unsqueeze(1).to_broadcast([128, 4, 128]),
                      ALU.mult)
        b.free = [z]
        self.P.wait(z, unit["v", 0], unit["v", 1])
        for t in range(2):
            b = self.banks[1 + t]
            self.P.wait(b.free)
            for g in range(4):
                self.P.mm(b.ap[:, g * 128:(g + 1) * 128], wT[:, g, :], va[:, t, g * 128:(g + 1) * 128], True, True)
            tk = self.P.done()
            self.V.wait(tk, jt)
            for g in range(4):
                sl = slice(g * 128, (g + 1) * 128)
                f = self.V.stt(y[:, t, sl], b.ap[:, sl], self.vc[:, 89 + g:90 + g], u[:, t, sl], ALU.add, ALU.mult)
            b.free = [f]
        sp, lf, c8 = self.al2(2, 8), self.al2(2, 8), self.al2(2, 8)
        self.V.wait(jt)
        z = self.V.tt(lf, f8, fb.unsqueeze(1).to_broadcast([128, 2, 8]), ALU.add)
        z = self.V.ts(lf, lf, -1.0, None, ALU.mult, None)
        self.S.wait(z)
        z = self.S.ac(sp, lf, ACT.Abs)
        z = self.S.ac(sp, sp, ACT.Exp, scale=-1.0)
        self.V.wait(z)
        z = self.V.ts(sp, sp, 1.0, None, ALU.add, None)
        self.S.wait(z)
        z = self.S.ac(sp, sp, ACT.Ln)
        self.V.wait(z)
        z = self.V.stt(lf, lf, 0.0, sp, ALU.max, ALU.add)
        z = self.V.ts(lf, lf, -1.0, None, ALU.mult, None)
        b = self.banks[3]
        self.P.wait(z, b.free)
        self.P.mm(b.ap[:, 0:8], self.const("le"), lf[:, 0, :], True, True)
        self.P.mm(b.ap[:, 8:16], self.const("ones"), lf[:, 0, :], True, False)
        self.P.mm(b.ap[:, 8:16], self.const("le"), lf[:, 1, :], False, True)
        tk = self.P.done()
        self.V.wait(tk)
        z = self.V.cp(c8, b.ap[:, 0:16].rearrange("p (t h) -> p t h", t=2))
        self.P.wait(z)
        for t in range(2):
            self.P.tr(b.ap[0:8, 128 + t * 128:256 + t * 128], c8[:, t, :])
        tk = self.P.done()
        cT = self.al(256)
        self.V.wait(tk)
        z = self.V.ts(cT[0:8, :], b.ap[0:8, 128:384], -1.0, None, ALU.mult, None)
        b.free = [z]
        ctk = z
        sel = self.al2(8, 128)
        so = self.off["sel"][0]
        slt = self.misc(sel[0:8], self.i["consts"][0:8, so:so + 1024].rearrange("p (a b) -> p a b", a=8))
        Ss = [self.al(256) for _ in range(2)]
        self.P.wait(turned, ctk, slt, jt)
        self.V.wait(lt)

        def scores(n, ex):
            t, h = n // 8, n % 8
            nk = 128 * (t + 1)
            b = self.banks[n % 2]
            r0 = 64 * (h % 2)
            self.P.wait(b.free)
            self.P.mm(b.ap[:, 0:nk], qT[r0:r0 + 64, h // 2, t * 128:(t + 1) * 128], kT[r0:r0 + 64, h // 2, 0:nk], True, False)
            self.P.mm(b.ap[:, 0:nk], sel[0:8, h, :], cT[0:8, 0:nk], False, True)
            self.V.wait(self.P.done(), ex.get(n - 2))
            f = self.V.stt(Ss[n % 2][:, 0:nk], b.ap[:, 0:nk], c8[:, t, h:h + 1], causal[:, t, 0:nk], ALU.add, ALU.add)
            b.free = [f]
            return Ss[n % 2][:, 0:nk], f, None

        f = self.attend(scores, lambda n: 128 * (n // 8 + 1), lambda n, c: vb[:, c, n % 8 * 64:(n % 8 + 1) * 64], 1.0,
                        lambda n: y[:, n // 8, 512 + n % 8 * 64:512 + (n % 8 + 1) * 64])
        yT = self.al2(8, 256)
        for t in range(2):
            z = self.to_T(y[:, t, :], 8, yT[:, :, t * 128:(t + 1) * 128], f)
        self.proj_tok(yT, 8, self.i["ev_w_out_2"][0], 1024, 2, self.add_x, z)

    def add_x(self, t, n0, nw, b, tk):
        x = self.X[:, t + 2, n0:n0 + nw]
        self.V.wait(tk)
        return self.V.tt(x, x, b[:, 0:nw], ALU.add)

    def ffn(self, l):
        self.stage()
        hT = self.al2(8, 256)
        scr = self.al(3080)
        ht = self.norm_T([2, 3], hT, self.gain_cols("norm_ffn_2", l), None, scr)
        steps = iter(())
        if l == 0:
            steps = self.tables = self.s5_tables()
            next(steps)
            self.V.wait(self.P.done())
        cr = self.al(5632)
        cw = self.al2(44, 4)
        lane = Lane(self.sem(f"l_ffn{l}"))
        self.G.dma(lane, cr[0:3, :], self.i["ffn_conv_w_2"][l])
        t = self.G.dma(lane, cr[3:4, :], self.i["ffn_conv_b_2"][l].unsqueeze(0))
        b = self.banks[7]
        self.P.wait(t, b.free)
        for c in range(44):
            self.P.tr(b.ap[:, c * 4:c * 4 + 4], cr[0:4, c * 128:(c + 1) * 128])
        tk = self.P.done()
        self.V.wait(tk)
        cwt = self.V.cp(cw, b.ap[:, 0:176].rearrange("p (a b) -> p a b", a=44))
        b.free = [cwt]
        aT = self.al2(22, 256)
        accs = [self.al(256) for _ in range(3)]
        af = [None] * 3

        def cb(c, bank, tk):
            a = accs[c % 3]
            self.V.wait(tk, af[c % 3], cwt)
            z = self.V.ts(a, bank[:, 0:256], cw[:, c, 2:3], cw[:, c, 3:4], ALU.mult, ALU.add, apart=True)
            z = self.V.stt(a[:, 1:256], bank[:, 0:255], cw[:, c, 1:2], a[:, 1:256], ALU.mult, ALU.add)
            z = self.V.stt(a[:, 2:256], bank[:, 0:254], cw[:, c, 0:1], a[:, 2:256], ALU.mult, ALU.add)
            if c < 22:
                self.S.wait(z)
                af[c % 3] = self.S.ac(aT[:, c, :], a, ACT.Silu)
            else:
                self.V.wait(self.S.last)
                af[c % 3] = self.V.tt(aT[:, c - 22, :], aT[:, c - 22, :], a, ALU.mult)
            for _ in range(0 if c < 3 else 2 if c < 30 else 1):
                next(steps, None)
            return z

        self.proj_feat(hT, 8, self.i["ffn_w_up_2"][l], 5632, 256, cb, ht, banks=self.banks[0:4])
        at = self.V.last
        self.proj_tok(aT, 22, self.i["ffn_w_down_2"][l], 1024, 2, self.add_x, at, banks=self.banks[4:8])

    def ple(self, l):
        self.stage()
        hT = self.al2(8, 256)
        scr = self.al(3080)
        one = self.const("ones")[:, 0:8]
        ht = self.norm_T([2, 3], hT, [one, one], None, scr)
        p = self.al2(2, 256)
        pT = self.al2(2, 256)
        lt = self.misc(p, self.i["p_2"][l, 0].rearrange("(t p) d -> p t d", p=128))
        for t in range(2):
            z = self.to_T(p[:, t, :], 2, pT[:, :, t * 128:(t + 1) * 128], lt)
        pr = self.al2(2, 1024)

        def pcols(t, n0, nw, b, tk):
            self.V.wait(tk)
            return self.V.cp(pr[:, t, n0:n0 + nw], b)

        self.proj_tok(pT, 2, self.i["ple_w_proj_2"][l], 1024, 2, pcols, z)
        gt = [self.al(512) for _ in range(2)]
        gf = [None, None]

        def cb(t, n0, nw, b, tk):
            self.S.wait(tk, gf[t])
            z = self.S.ac(gt[t], b, ACT.Sigmoid)
            self.V.wait(z)
            self.V.tt(gt[t], gt[t], pr[:, t, n0:n0 + nw], ALU.mult)
            x = self.X[:, t + 2, n0:n0 + nw]
            gf[t] = self.V.tt(x, x, gt[t], ALU.add)
            return z

        self.proj_tok(hT, 8, self.i["ple_w_gate_2"][l], 1024, 2, cb, ht)

    def s5_tables(self):
        V, S, G = self.V, self.S, self.G
        M, AD, SU = ALU.mult, ALU.add, ALU.subtract
        back, self.top = self.top, 20520
        par = self.al2(3, 32)
        mag, th, k, sn, cs, t1, t2, den, cr, ci, nr, ni = (self.al(32) for _ in range(12))
        Er, Ei = self.al2(32, 256), self.al2(32, 256)
        BT = [self.al2(8, 128) for _ in range(2)]
        CT = [self.al2(8, 128) for _ in range(2)]
        self.s5t = mag, Er, Ei, BT, CT
        self.top = 17340
        rows, ld = self.al2(3, 128), self.al(2)
        bre, bim = self.al2(32, 16), self.al2(32, 16)
        cc = [self.al2(8, 64) for _ in range(2)]
        t16 = [self.al2(32, 16)]
        assert self.top <= 20520
        self.top = 2048
        t16.append(self.al2(32, 16))
        bb, cz = self.al3(32, 2, 16), self.al3(8, 2, 64)
        assert self.top <= 2048 + 3080
        self.top = 2048
        tm = [self.al(1024) for _ in range(2)]
        self.top = back
        banks = self.banks[4:7]
        lane = Lane(self.sem("l_s5"))
        G.dma(lane, rows[0:32, 0, :], self.i["od_a_re_2"][0].rearrange("(j g) p -> j (g p)", g=2))
        G.dma(lane, rows[0:32, 1, :], self.i["od_a_im_2"][0].rearrange("(j g) p -> j (g p)", g=2))
        lt = G.dma(lane, ld[0:32, :], self.i["od_log_dt_2"][0].rearrange("(j g) -> j g", g=2))
        lane = Lane(self.sem("l_s5b"))
        G.dma(lane, bre, self.i["od_b_re_2"][0].rearrange("(j g) p c -> (g p) j c", g=2))
        lb = G.dma(lane, bim, self.i["od_b_im_2"][0].rearrange("(j g) p c -> (g p) j c", g=2))
        lane = Lane(self.sem("l_s5c"))
        G.dma(lane, cc[0], self.i["od_c_re_2"][0].rearrange("(q g) c p -> (g c) q p", g=8))
        lc = G.dma(lane, cc[1], self.i["od_c_im_2"][0].rearrange("(q g) c p -> (g c) q p", g=8))
        yield
        V.wait(lt)
        z = V.cp(rows[0:32, 2, :].rearrange("p (g s) -> p g s", g=2), ld[0:32, :].unsqueeze(2).to_broadcast([32, 2, 64]))
        b = banks[0]
        self.P.wait(lt, z, b.free)
        for n in range(3):
            self.P.tr(b.ap[:, n * 32:(n + 1) * 32], rows[0:32, n, :])
        tk = self.P.done()
        V.wait(tk)
        z = V.cp(par, b.ap[:, 0:96].rearrange("p (a b) -> p a b", a=3))
        b.free = [z]
        yield
        lr, li, dt = par[:, 0, :], par[:, 1, :], par[:, 2, :]
        S.wait(z)
        z = S.ac(dt, dt, ACT.Exp)
        V.wait(z)
        z = V.tt(mag, lr, dt, M)
        S.wait(z)
        zm = S.ac(mag, mag, ACT.Exp)
        V.tt(th, li, dt, M)
        V.ts(k, th, float(1 / (2 * np.pi)), 12582912.0, M, AD)
        V.ts(k, k, 12582912.0, None, SU, None)
        yield
        c1 = 6.28125
        V.stt(th, k, -c1, th, M, AD)
        V.stt(th, k, float(-(2 * np.pi - c1)), th, M, AD)
        lim = 3.1415925
        z = V.ts(th, th, lim, -lim, ALU.min, ALU.max)
        S.wait(z)
        S.ac(sn, th, ACT.Sin)
        z = S.ac(cs, th, ACT.Abs)
        yield
        V.wait(z)
        z = V.ts(cs, cs, -1.0, float(np.pi / 2), M, AD)
        S.wait(z)
        z = S.ac(cs, cs, ACT.Sin)
        V.wait(z, zm)
        V.tt(nr, mag, cs, M)
        V.ts(nr, nr, -1.0, None, AD, None)
        V.tt(ni, mag, sn, M)
        V.tt(den, lr, lr, M)
        yield
        V.tt(t1, li, li, M)
        V.tt(den, den, t1, AD)
        V.rec(den, den)
        for dst, a, c, op in ((cr, nr, ni, AD), (ci, ni, nr, SU)):
            V.tt(t1, a, lr, M)
            V.tt(t2, c, li, M)
            V.tt(dst, t1, t2, op)
            V.tt(dst, dst, den, M)
            yield
        crb, cib = cr.unsqueeze(2).to_broadcast([128, 32, 16]), ci.unsqueeze(2).to_broadcast([128, 32, 16])
        pm = self.const("par")
        z2 = None
        V.wait(lb)
        for n, (a, c, op) in enumerate(((bre, bim, SU), (bim, bre, AD))):
            V.tt(t16[0], a, crb, M)
            V.tt(t16[1], c, cib, M)
            V.tt(t16[0], t16[0], t16[1], op)
            yield
            V.wait(z2)
            for g2 in range(2):
                z = V.ts(bb[:, :, g2, :], t16[0], pm[:, 2 + g2:3 + g2], None, M, None)
            yield
            z2 = self.to_T(bb.rearrange("p j g c -> p (j g c)"), 8, BT[n], z, banks)
            yield
        V.wait(lc)
        for n in range(2):
            V.wait(z2)
            for g2 in range(2):
                z = V.ts(cz[:, :, g2, :], cc[n], pm[:, g2:g2 + 1], (1.0, -1.0)[n], M, M)
            yield
            z2 = self.to_T(cz.rearrange("p q g s -> p (q g s)"), 8, CT[n], z, banks)
            yield
        V.wait(z2)
        V.ms(Er[:, :, 0:1], 1.0)
        V.ms(Ei[:, :, 0:1], 0.0)
        V.cp(Er[:, :, 1], cs)
        V.cp(Ei[:, :, 1], sn)
        yield
        for q in range(1, 8):
            w = 1 << q
            half = w // 2
            hr, hi = Er[:, :, half], Ei[:, :, half]
            V.tt(t1, hr, hr, M)
            V.tt(t2, hi, hi, M)
            V.tt(Er[:, :, w], t1, t2, SU)
            V.tt(t1, hr, hi, M)
            V.ts(Ei[:, :, w], t1, 2.0, None, M, None)
            yield
            nj = min(32, 1024 // w)
            for j0 in range(0, 32, nj):
                j = slice(j0, j0 + nj)
                wr = Er[:, j, w:w + 1].to_broadcast([128, nj, w - 1])
                wi = Ei[:, j, w:w + 1].to_broadcast([128, nj, w - 1])
                m = [a[:, 0:nj * (w - 1)].rearrange("p (j t) -> p j t", j=nj) for a in tm]
                for dst, x, y_, op in ((Er, Er, Ei, SU), (Ei, Ei, Er, AD)):
                    V.tt(m[0], x[:, j, 1:w], wr, M)
                    if w >= 32:
                        yield
                    V.tt(m[1], y_[:, j, 1:w], wi, M, apart=True)
                    if w >= 32:
                        yield
                    V.tt(dst[:, j, w + 1:2 * w], m[0], m[1], op)
                    yield

    def s5(self):
        self.stage()
        V, S, G = self.V, self.S, self.G
        M, AD, SU = ALU.mult, ALU.add, ALU.subtract
        hT = self.al2(8, 256)
        scr = self.al(3080)
        if self.tables is None:
            self.tables = self.s5_tables()
        for _ in self.tables:
            pass
        mag, Er, Ei, BT, CT = self.s5t
        ht = self.norm_T([2, 3], hT, self.gain_cols("norm_mix_2", 1), None, scr, dep=[V.last, self.P.done()])
        z2 = [V.last, S.last]
        tm = [self.al(32 * 128) for _ in range(2)]
        assert self.top <= 20520
        gy = scr[:, 0:2048].rearrange("p (k t) -> p k t", k=8)
        a1 = [tm[0][:, n * 1024:n * 1024 + 512].rearrange("p (c t) -> p c t", c=2) for n in range(4)]
        a2 = [tm[0][:, n * 1024 + 512:n * 1024 + 1024].rearrange("p (c t) -> p c t", c=2) for n in range(4)]
        w2 = [tm[1][:, n * 1024:n * 1024 + 512].rearrange("p (c t) -> p c t", c=2) for n in range(4)]
        x2 = [tm[1][:, n * 1024 + 512:n * 1024 + 1024].rearrange("p (c t) -> p c t", c=2) for n in range(4)]
        xfree, pool, done = [None] * 4, [None] * 4, {}
        two = lambda a: a.unsqueeze(1).to_broadcast([128, 2, 256])

        def drive(j):
            q, jj = j // 4, j % 4
            rs = slice(32 * jj, 32 * jj + 32)
            b = self.banks[j % 4]
            self.P.wait(z2, ht, b.free)
            for n in range(2):
                self.P.mm(b.ap[:, n * 256:(n + 1) * 256], BT[n][rs, q, :], hT[rs, q, :], True, True, at=(32 * jj, 0))
            tk = self.P.done()
            b.done = tk

        drive(0)
        drive(1)
        self.P.wait(z2)
        for j in range(32):
            q, jj = j // 4, j % 4
            yb = self.banks[4 + q % 2]
            rs = slice(32 * jj, 32 * jj + 32)
            b = self.banks[j % 4]
            if j + 2 < 32:
                drive(j + 2)
            bv = b.ap.rearrange("p (c t) -> p c t", c=2)
            er, ei = Er[:, j, :], Ei[:, j, :]
            A_, B_, w_, x_ = a1[jj], a2[jj], w2[jj], x2[jj]
            V.wait(b.done, pool[jj])
            V.tt(A_, bv, two(er), M, apart=True)
            z = V.tt(B_, bv, two(ei), M, apart=True)
            b.free = [z]
            V.tt(A_[:, 0, :], A_[:, 0, :], B_[:, 1, :], AD)
            V.tt(A_[:, 1, :], A_[:, 1, :], B_[:, 0, :], SU, apart=True)
            mg = mag[:, j:j + 1].to_broadcast([128, 256])
            for n in range(2):
                z = V.scan(w_[:, n, :], mg, A_[:, n, :], apart=n == 1)
            G.wait(z)
            G.tt(A_, w_, two(er), M)
            z = V.tt(B_, w_, two(ei), M)
            G.wait(z, xfree[jj])
            G.tt(x_[:, 0, :], A_[:, 0, :], B_[:, 1, :], SU)
            z = G.tt(x_[:, 1, :], A_[:, 1, :], B_[:, 0, :], AD, apart=True)
            pool[jj] = z
            self.P.wait(z, yb.free)
            for n in range(2):
                self.P.mm(yb.ap[rs, 0:256], CT[n][:, q, rs], x_[:, n, :], n == 0, n == 1, at=(0, 32 * jj))
            tk = self.P.done()
            xfree[jj] = tk
            if jj == 3:
                done[q] = tk
            for c in ([q - 1] if jj == 1 and q else []) + ([7] if j == 31 else []):
                yc = self.banks[4 + c % 2]
                self.V.wait(done[c])
                z = self.V.stt(gy[:, c, :], hT[:, c, :], self.vec("od_d_2", 0)[:, c:c + 1], yc.ap[:, 0:256], M, AD)
                yc.free = [z]
        self.S.wait(z)
        z = self.S.ac(gy, gy, ACT.Gelu_apprx_tanh)
        ga = Er.rearrange("p j t -> p (j t)")[:, 0:2048].rearrange("p (t d) -> p t d", t=2)
        sg = [Ei.rearrange("p j t -> p (j t)")[:, n * 512:(n + 1) * 512] for n in range(2)]
        gf = [None, None]

        def cb(t, n0, nw, b, tk):
            if n0 < 1024:
                self.V.wait(tk)
                return self.V.cp(ga[:, t, n0:n0 + nw], b)
            n1 = n0 - 1024
            self.S.wait(tk, gf[t])
            z = self.S.ac(sg[t], b, ACT.Sigmoid)
            self.V.wait(z)
            self.V.tt(sg[t], sg[t], ga[:, t, n1:n1 + nw], ALU.mult)
            x = self.X[:, t + 2, n1:n1 + nw]
            gf[t] = self.V.tt(x, x, sg[t], ALU.add)
            return z

        self.S.wait(self.V.last)
        self.proj_tok(gy, 8, self.i["od_w_glu_2"][0], 2048, 2, cb, z)

    def end(self):
        self.stage()
        lane = Lane(self.sem("l_out"))
        self.SP.wait(self.V.last)
        t = self.SP.dma(lane, self.out[0].rearrange("(t p) d -> p t d", p=128), self.X[:, 2:4, :])
        self.SP.wait(t)

    def run(self):
        block = self.ctx.enter_context(self.nc.Block())

        @block.tensor
        def _(e):
            self.P.emit(e)

        @block.vector
        def _(e):
            self.V.emit(e)

        @block.scalar
        def _(e):
            self.S.emit(e)

        @block.gpsimd
        def _(e):
            self.G.emit(e)

        @block.sync
        def _(e):
            self.SP.emit(e)


def build(nc, ins, out, stages=None):
    with ExitStack() as ctx:
        p = Model(nc, ins, out, ctx)
        p.begin()
        p.ng = p.vc[:, 88:89]
        for name, args in (("ada", ()), ("deltanet", ()), ("peer", (0, (0, 1))), ("peer", (0, (2, 3))), ("attention", ()),
                           ("peer", (1, (2, 3))), ("final_norm", ()), ("even_mixer", ()), ("ffn", (0,)), ("ple", (0,)),
                           ("s5", ()), ("ffn", (1,)), ("ple", (1,))):
            if stages is None or name in stages:
                {"ada": p.ada, "deltanet": p.deltanet, "peer": p.peer, "attention": p.attention,
                 "final_norm": p.final_norm, "even_mixer": p.even_mixer, "ffn": p.ffn, "ple": p.ple, "s5": p.s5}[name](*args)
        p.end()
        p.run()


_INS = ["x", "c", "ctx", "c_ctx", "ada_w", "ada_b", "norm1_g", "norm2_g", "final_g", "dn_w_in", "dn_conv_w", "dn_a_log",
        "dn_dt_bias", "dn_norm_g", "dn_w_out", "att_w_in", "att_qn_g", "att_kn_g", "att_w_out", "peer_w_query",
        "peer_sub_keys", "peer_u", "peer_v", "p_2", "norm_mix_2", "norm_ffn_2", "ev_w_in_2", "ev_b_fgate_2",
        "ev_q_norm_2", "ev_k_norm_2", "ev_v_norm_2", "ev_w_spatial_2", "ev_b_spatial_2", "ev_w_out_2", "od_a_re_2",
        "od_a_im_2", "od_log_dt_2", "od_b_re_2", "od_b_im_2", "od_c_re_2", "od_c_im_2", "od_d_2", "od_w_glu_2",
        "ffn_w_up_2", "ffn_conv_w_2", "ffn_conv_b_2", "ffn_w_down_2", "ple_w_proj_2", "ple_w_gate_2"]


def kernel(**inputs):
    import concourse.bacc as _bacc
    from concourse.bass_utils import run_bass_kernel_spmd as _run

    nc = _bacc.Bacc("TRN2", target_bir_lowering=False, num_devices=1)
    arrays, args = {}, {}
    given = {name: np.ascontiguousarray(inputs[name]) for name in _INS}
    given["consts"] = constants()[0]
    for name, a in given.items():
        arrays[f"in_{name}"] = a
        args[name] = nc.dram_tensor(f"in_{name}", a.shape, mybir.dt.from_np(a.dtype), kind="ExternalInput").ap()
    out = nc.dram_tensor("out_0", (1, 256, 1024), F32, kind="ExternalOutput").ap()
    build(nc, args, out)
    r = _run(nc, [arrays], core_ids=[0])
    return r.results[0]["out_0"]
```
